# Optimizing a Trainium2 kernel written in Bass

```python
import jax, jax.numpy as jnp
from jax import lax
import numpy as np

D_MODEL = 2048
BATCH = 1
SEQ = 1024
DEPTH = 1

RET_HEADS = 4
RET_DK = 128
RET_DV = 256
RET_WIDTH = RET_HEADS * RET_DV
HG_HEADS = 8
HG_DK = 128
HG_DV = 128
HG_WIDTH = HG_HEADS * HG_DV
MIX_WIDTH = RET_WIDTH + HG_WIDTH
RET_CHUNK = 128
HG_CHUNK = 64
ROPE_BASE = 10000.0
EPS = 1e-6
ALPHA = (2.0 * DEPTH) ** 0.25
BETA = (8.0 * DEPTH) ** -0.25
RET_LOG2_DECAY = tuple(5.0 + 7.0 * h / (RET_HEADS - 1) for h in range(RET_HEADS))
SPLITS = (RET_HEADS * RET_DK, RET_HEADS * RET_DK, RET_WIDTH, RET_WIDTH,
          HG_HEADS * HG_DK, HG_HEADS * HG_DK, HG_WIDTH, HG_WIDTH)
IN_WIDTH = sum(SPLITS)
SPLIT_POINTS = [int(v) for v in np.cumsum(SPLITS)[:-1]]

kernel_name = "hymba_retnet_hgrn2_deepnorm_adaln"

def _layernorm_noaffine(x):
    xf = x.astype(jnp.float32)
    mu = jnp.mean(xf, axis=-1, keepdims=True)
    var = jnp.mean(jnp.square(xf - mu), axis=-1, keepdims=True)
    return (xf - mu) * lax.rsqrt(var + EPS)

def _rmsnorm(x):
    xf = x.astype(jnp.float32)
    return xf * lax.rsqrt(jnp.mean(jnp.square(xf), axis=-1, keepdims=True) + EPS)

def _rotary(x, positions):
    half = x.shape[-1] // 2
    freqs = ROPE_BASE ** (-jnp.arange(half, dtype=jnp.float32) / half)
    ang = positions.astype(jnp.float32)[..., None] * freqs
    cos = jnp.cos(ang)[:, :, None, :]
    sin = jnp.sin(ang)[:, :, None, :]
    x1, x2 = x[..., :half], x[..., half:]
    return jnp.concatenate([x1 * cos - x2 * sin, x1 * sin + x2 * cos], axis=-1).astype(x.dtype)

def _retention(q, k, v):
    B, T, H, DK = q.shape
    DV = v.shape[-1]
    C = RET_CHUNK
    N = T // C
    lg = jnp.log1p(-jnp.exp2(-jnp.asarray(RET_LOG2_DECAY, jnp.float32)))
    idx = jnp.arange(C, dtype=jnp.float32)
    diff = idx[:, None] - idx[None, :]
    causal = diff >= 0
    d_intra = jnp.where(causal, jnp.exp(jnp.where(causal, diff, 0.0)[None] * lg[:, None, None]), 0.0)
    qc = q.reshape(B, N, C, H, DK)
    kc = k.reshape(B, N, C, H, DK)
    vc = v.reshape(B, N, C, H, DV)
    scores = jnp.einsum('bnihd,bnjhd->bnhij', qc, kc) * d_intra
    intra = jnp.einsum('bnhij,bnjhe->bnihe', scores, vc)
    zeta = jnp.exp((C - 1 - idx)[None, :] * lg[:, None])
    kv = jnp.einsum('bnjhd,hj,bnjhe->nbhde', kc, zeta, vc)
    chunk_decay = jnp.exp(C * lg)[None, :, None, None]

    def step(state, kv_n):
        return chunk_decay * state + kv_n, state

    _, s_prev = lax.scan(step, jnp.zeros((B, H, DK, DV), kv.dtype), kv)
    xi = jnp.exp((idx + 1)[None, :] * lg[:, None])
    inter = jnp.einsum('bnihd,hi,nbhde->bnihe', qc, xi, s_prev)
    return (intra + inter).reshape(B, T, H, DV)

def _hgrn2(q, f_pre, v, lb):
    B, T, H, DK = q.shape
    DV = v.shape[-1]
    C = HG_CHUNK
    N = T // C
    fp = f_pre.astype(jnp.float32)
    log_f = jnp.log(lb + (1.0 - lb) * jax.nn.sigmoid(fp))
    k = (1.0 - lb) * jax.nn.sigmoid(-fp)

    def to_chunks(a):
        return a.reshape(B, N, C, H, a.shape[-1]).swapaxes(0, 1)

    causal = jnp.tril(jnp.ones((C, C), bool))[None, :, :, None, None]

    def step(state, xs):
        qn, kn, vn, gn = xs
        b = jnp.cumsum(gn, axis=1)
        rel = jnp.exp(jnp.where(causal, b[:, :, None] - b[:, None, :], -jnp.inf))
        attn = jnp.einsum('bthd,bshd,btshd->bhts', qn, kn, rel)
        intra = jnp.einsum('bhts,bshe->bthe', attn, vn)
        inter = jnp.einsum('bthd,bhde->bthe', qn * jnp.exp(b), state)
        b_last = b[:, -1]
        new_state = (jnp.exp(b_last)[..., None] * state
                     + jnp.einsum('bshd,bshe->bhde', kn * jnp.exp(b_last[:, None] - b), vn))
        return new_state, intra + inter

    xs = (to_chunks(q.astype(jnp.float32)), to_chunks(k), to_chunks(v.astype(jnp.float32)), to_chunks(log_f))
    _, out = lax.scan(step, jnp.zeros((B, H, DK, DV), jnp.float32), xs)
    return out.swapaxes(0, 1).reshape(B, T, H, DV)

def setup_inputs(seed: int = 0) -> dict:
    key = jax.random.key(seed)
    ks = jax.random.split(key, 12)
    f32 = jnp.float32
    x = jax.random.normal(ks[0], (BATCH, SEQ, D_MODEL), f32)
    c = jax.random.normal(ks[1], (BATCH, D_MODEL), f32)
    offset = jax.random.randint(ks[2], (BATCH, 1), 0, 1024, dtype=jnp.int32)
    positions = (offset + jnp.arange(SEQ, dtype=jnp.int32)[None, :]).astype(jnp.int32)
    w_ada = 0.5 * D_MODEL ** -0.5 * jax.random.normal(ks[3], (DEPTH, D_MODEL, 3 * D_MODEL), f32)
    b_ada = 0.01 * jax.random.normal(ks[4], (DEPTH, 3 * D_MODEL), f32)
    col_scale = jnp.asarray(np.concatenate([
        np.full(n, BETA if j in (2, 6) else 1.0, np.float32) for j, n in enumerate(SPLITS)]))
    w_in = D_MODEL ** -0.5 * jax.random.normal(ks[5], (DEPTH, D_MODEL, IN_WIDTH), f32) * col_scale
    lb_logits = 0.1 * jax.random.normal(ks[6], (DEPTH + 1, HG_HEADS * HG_DK), f32)
    hg_norm_w = 1.0 + 0.02 * jax.random.normal(ks[7], (DEPTH, HG_WIDTH), f32)
    w_out = BETA * MIX_WIDTH ** -0.5 * jax.random.normal(ks[8], (DEPTH, MIX_WIDTH, D_MODEL), f32)
    ln_w = 1.0 + 0.02 * jax.random.normal(ks[9], (DEPTH, D_MODEL), f32)
    ln_b = 0.02 * jax.random.normal(ks[10], (DEPTH, D_MODEL), f32)
    return {"x": x, "c": c, "positions": positions, "w_ada": w_ada, "b_ada": b_ada,
            "w_in": w_in, "lb_logits": lb_logits, "hg_norm_w": hg_norm_w, "w_out": w_out,
            "ln_w": ln_w, "ln_b": ln_b}

def reference(x, c, positions, w_ada, b_ada, w_in, lb_logits, hg_norm_w, w_out, ln_w, ln_b):
    B, T, _ = x.shape
    lb_all = jnp.cumsum(jax.nn.softmax(lb_logits.astype(jnp.float32), axis=0), axis=0)
    cond = jax.nn.silu(c)
    for l in range(DEPTH):
        mod = cond @ w_ada[l] + b_ada[l]
        shift, scale, gate = jnp.split(mod, 3, axis=-1)
        h = (_layernorm_noaffine(x) * (1.0 + scale[:, None]) + shift[:, None]).astype(x.dtype)
        proj = h @ w_in[l]
        rq, rk, rv, rg, hq, hf, hi, hg = jnp.split(proj, SPLIT_POINTS, axis=-1)
        rq = _rotary(rq.reshape(B, T, RET_HEADS, RET_DK), positions) * (RET_DK ** -0.5)
        rk = _rotary(rk.reshape(B, T, RET_HEADS, RET_DK), positions)
        ret = _retention(rq, rk, rv.reshape(B, T, RET_HEADS, RET_DV))
        ret = _rmsnorm(ret).reshape(B, T, RET_WIDTH) * jax.nn.silu(rg.astype(jnp.float32))
        lb = lb_all[l].reshape(HG_HEADS, HG_DK)
        hgo = _hgrn2(hq.reshape(B, T, HG_HEADS, HG_DK), hf.reshape(B, T, HG_HEADS, HG_DK),
                     hi.reshape(B, T, HG_HEADS, HG_DV), lb)
        hgo = (_rmsnorm(hgo) * hg_norm_w[l].reshape(HG_HEADS, HG_DV)).reshape(B, T, HG_WIDTH)
        hgo = hgo * jax.nn.silu(hg.astype(jnp.float32))
        mixed = jnp.concatenate([ret, hgo], axis=-1).astype(x.dtype)
        y = mixed @ w_out[l]
        z = ALPHA * x + gate[:, None] * y
        x = (_layernorm_noaffine(z) * ln_w[l] + ln_b[l]).astype(x.dtype)
    return x


_drawn_inputs = setup_inputs


def setup_inputs(seed=0):
    import zlib

    import numpy as np

    out = dict(_drawn_inputs(seed))
    spreads = {}
    factors = {'b_ada': 8.0, 'lb_logits': 8.0, 'hg_norm_w': 8.0, 'ln_w': 2.787, 'ln_b': 2.86}
    for name, (base, spread) in spreads.items():
        noise = np.random.default_rng([zlib.crc32(name.encode()), seed]).standard_normal(out[name].shape)
        drawn = base * np.exp(spread * noise) if base else spread * noise
        out[name] = __import__('jax').numpy.asarray(drawn.astype(out[name].dtype))
    for name, factor in factors.items():
        out[name] = (out[name] * factor).astype(out[name].dtype)
    return out
```

```python
from contextlib import ExitStack

import numpy as np

import concourse.bass as bass
from concourse import mybir

ACT = mybir.ActivationFunctionType
ALU = mybir.AluOpType
F32 = mybir.dt.float32
F32R = mybir.dt.float32r
U8 = mybir.dt.uint8
I32 = mybir.dt.int32
ds = bass.ds

P = 128
T, D = 1024, 2048
NT, NK = T // P, D // P
RET_HEADS, RET_DV = 4, 256
HG_HEADS = 8
PAIRS = HG_HEADS // 2
EPS = 1e-6
ALPHA = 2.0 ** 0.25
C_RQ, C_RK, C_RV, C_RG, C_HQ, C_HF, C_HI, C_HG = 0, 512, 1024, 2048, 3072, 4096, 5120, 6144
LEVELS = (64, 32, 16, 8, 4, 2, 1)
NL = len(LEVELS)
STEPS = 8
RING = 4
RET_PANELS = 3 * RET_HEADS
PANELS = RET_PANELS + 4 * PAIRS
BSTEPS = 16
LEAD = 3

A_GEN = {0: 2, 1: 3, 2: 10, 3: 12}
B_GEN = {0: 2, 1: 3, 2: 6, 3: 8}
A_SCORE = {8 + c: c for c in range(8)}
B_SCORE = {4: 0, 5: 1, 6: 2, 7: 3, 9: 4, 10: 5, 11: 6, 12: 7}
A_APPLY = {s + 1: c for s, c in A_SCORE.items()}
B_APPLY = {s + 1: c for s, c in B_SCORE.items()}
A_NORM, A_MIX = {17: 0, 18: 1}, {25: 0, 26: 1}
B_NORM, B_MIX = {8: 0, 14: 1}, {11: 0, 14: 1}


def constants():
    i = np.arange(P)
    gamma = 1.0 - 2.0 ** -(5.0 + 7.0 * np.arange(RET_HEADS) / (RET_HEADS - 1))
    scale = float(P) ** -0.5
    diff = (i[None, :] - i[:, None]).astype(np.float64)
    decay = [np.where(diff >= 0, g ** np.maximum(diff, 0), 0.0) * scale for g in gamma]
    q_decay = [np.broadcast_to(g ** (i + 1.0) * scale, (P, P)) for g in gamma]
    k_decay = np.stack([g ** (P - 1.0 - i) for g in gamma], 1)
    chunk_decay = np.broadcast_to(gamma ** float(P), (P, RET_HEADS))
    freq = (10000.0 ** (-np.arange(64) / 64.0))[i % 64][:, None]
    sign = np.where(i < 64, 1.0, -1.0)[:, None]
    table = np.concatenate([np.eye(P), *decay, *q_decay, k_decay, chunk_decay, freq, sign], 1).astype(np.float32)
    s, t = i[:, None], i[None, :]
    masks = [((s // (2 * m) == t // (2 * m)) & (s // m % 2 == 0) & (t // m % 2 == 1)) for m in LEVELS[1:]]
    return np.ascontiguousarray(table), np.ascontiguousarray(np.concatenate(masks, 1).astype(np.uint8))


def hymba_layer(nc, x, c, positions, w_ada, b_ada, w_in, lb_logits, hg_norm_w, w_out, ln_w, ln_b, out):
    table_np, masks_np = constants()
    table_dram = nc.inline_tensor(table_np, "shape_tables").ap()
    masks_dram = nc.inline_tensor(masks_np, "level_masks").ap()
    mix_hi_dram = nc.dram_tensor("mixed_hi", (NK, P, T), F32, kind="Internal").ap()
    mix_lo_dram = nc.dram_tensor("mixed_lo", (NK, P, T), F32, kind="Internal").ap()
    gate_dram = nc.dram_tensor("gate_row", (1, D), F32, kind="Internal").ap()

    start = (nc.sbuf_base + 63) // 64 * 64

    def place(name, at, shape, dt=F32):
        size = (int(np.prod(shape[1:])) * (1 if dt == U8 else 4) + 31) // 32 * 32
        assert start + at + size <= nc.sbuf_usable_end, (name, start + at + size - nc.sbuf_usable_end)
        return nc.alloc_sbuf_tensor_at(name, list(shape), dt, offset=start + at), at + size

    KB = 1024
    h_hi, at = place("h_hi", 0, [P, NK, T], F32R)
    h_lo, at = place("h_lo", at, [P, NK, T], F32R)
    H_LO = 64 * KB
    ada_in = [place(f"ada_in{i}", i * 16 * KB, [P, 2 * D])[0] for i in range(3)]
    angle = place("angle", 48 * KB, [P, T])[0]
    turns = place("turns", 52 * KB, [P, T])[0]
    pos_i = place("pos_i", 56 * KB, [P, T], I32)[0]
    lnx_t = place("lnx_t", H_LO, [P, NK, T])[0]
    w_raw, _ = place("w_raw", at, [P, RING, 512])
    w_low, at = place("w_low", at, [P, RING, 512], F32R)
    w_high, at = place("w_high", at, [P, RING, 512], F32R)
    ident, at = place("ident", at, [P, P])
    ones, at = place("ones", at, [P, P])
    smalls_t, at = place("smalls_t", at, [P, 40])
    vecs, at = place("vecs", at, [P, 96])
    stats, at = place("stats", at, [P, 64])
    cond = vecs[:, 0:16]
    shift_t, scale1_t = vecs[:, 16:32], vecs[:, 32:48]
    lower, upper = vecs[:, 48:56], vecs[:, 56:64]
    lbtmp = vecs[:, 64:80]
    eps_t = vecs[:, 80:81]
    one_t = ones[:, 0:1]
    half_pi = vecs[:, 81:82]
    freq_t, sign_t = vecs[:, 82:83], vecs[:, 83:84]
    k_decay, chunk_decay = vecs[:, 84:88], vecs[:, 88:92]
    ln_upper = vecs[:, 64:72]
    head_vecs = vecs[:, 92:96]
    at_buf, at = place("at_buf", at, [P, 2, P])
    kt_buf, at = place("kt_buf", at, [P, 2, P])
    state, at = place("state", at, [P, RET_DV])
    tmp_hi, _ = place("tmp_hi", at, [P, 512], F32R)
    tmp_s, at = place("tmp_s", at, [P, 512])
    tmp_e, at = place("tmp_e", at, [P, 512])
    masks, at = place("masks", at, [P, (NL - 1) * P], U8)
    dec_t, at = place("dec_t", at, [P, 2, 2])
    A0 = at
    r_q, at = place("r_q", A0, [P, T])
    r_k, at = place("r_k", at, [P, T])
    r_qx, at = place("r_qx", at, [P, T])
    r_t, at = place("r_t", at, [P, T])
    V0 = at
    r_v, at = place("r_v", at, [P, NT, RET_DV])
    r_g, at = place("r_g", at, [P, 2, T])
    r_o, at = place("r_o", at, [P, 2, T])
    cos_t, at = place("cos_t", at, [P, T])
    sin_t, at = place("sin_t", at, [P, T])
    decay_m, at = place("decay_m", at, [P, RET_HEADS, P])
    q_decay_m, at = place("q_decay_m", at, [P, RET_HEADS, P])
    x_in = [place(f"x_in{i}", A0 + 8 * KB * i, [P, D])[0] for i in range(2)]
    ada_sum = place("ada_sum", V0, [P, 2 * D])[0]
    smalls = place("smalls", V0 + 16 * KB, [P, P])[0]
    h_tmp = place("h_tmp", A0, [P, 2, T])[0]
    gate_in = [place(f"gate_in{i}", V0 + 8 * KB * i, [P, D])[0] for i in range(2)]
    gate_sum = place("gate_sum", V0 + 16 * KB, [P, D])[0]
    gate_out = place("gate_out", V0, [P, D])[0]
    g_q, at = place("g_q", A0, [P, T])
    g_k, at = place("g_k", at, [P, T])
    g_b, at = place("g_b", at, [P, T])
    Z0 = at
    g_v, at = place("g_v", at, [P, NT, 256])
    g_g, at = place("g_g", at, [P, 2, T])
    g_o, at = place("g_o", at, [P, 2, T])
    lev, at = place("lev", at, [P, 2, NL + 1, 256])
    qe, at = place("qe", at, [P, 2, 256])
    gate_bc = place("gate_bc", A0, [P, D])[0]
    z, at = place("z", Z0, [P, 4, D])
    x_re, at = place("x_re", at, [P, 4, 512])
    late = place("late", 0, [P, NK, T])[0]
    lnw_bc, lnb_bc = late[:, 0:4, 0:512], late[:, 4:8, 0:512]

    main = nc.alloc_psum_tensor("main", [P, 4, 512], F32)
    sc0 = nc.alloc_psum_tensor("sc0", [P, 512], F32)
    sc1 = nc.alloc_psum_tensor("sc1", [P, 512], F32)
    ops = nc.alloc_psum_tensor("ops", [P, 512], F32)
    aux = nc.alloc_psum_tensor("aux", [P, 512], F32)

    ctx = ExitStack()

    def sem(name):
        return ctx.enter_context(nc.semaphore(name))

    tables_in, smalls_in, pos_in, sums_in = sem("tables_in"), sem("smalls_in"), sem("pos_in"), sem("sums_in")
    decay_in, gate_bias_in = sem("decay_in"), sem("gate_bias_in")
    x_loaded = [sem(f"x_loaded{i}") for i in range(2)]
    ada_loaded = [sem(f"ada_loaded{i}") for i in range(3)]
    gate_loaded = [sem(f"gate_loaded{i}") for i in range(2)]
    set_up = sem("set_up")
    x_stats = sem("x_stats")
    x_normed = sem("x_normed")
    x_turned = sem("x_turned")
    x_placed = sem("x_placed")
    smalls_turned, smalls_placed = sem("smalls_turned"), sem("smalls_placed")
    cond_exp, cond_ready, lb_diff, lb_exp = sem("cond_exp"), sem("cond_ready"), sem("lb_diff"), sem("lb_exp")
    lb_ready, ln_ready = sem("lb_ready"), sem("ln_ready")
    sums_zero = sem("sums_zero")
    ada_used = sem("ada_used")
    mod_done, mod_ready = sem("mod_done"), sem("mod_ready")
    angle_ready, trig_ready = sem("angle_ready"), sem("trig_ready")
    h_made = sem("h_made")
    h_ready = sem("h_ready")
    gate_used, gate_turned, gate_copied, gate_stored = (
        sem("gate_used"), sem("gate_turned"), sem("gate_copied"), sem("gate_stored"))
    w_loaded = [sem(f"w_loaded{i}") for i in range(RING)]
    w_hi_ready, w_lo_ready = sem("w_hi_ready"), sem("w_lo_ready")
    w_used = sem("w_used")
    bank_done = [sem(f"bank_done{i}") for i in range(4)]
    bank_read = [sem(f"bank_read{i}") for i in range(4)]
    rope_ready, qx_ready = sem("rope_ready"), sem("qx_ready")
    head_ready = sem("head_ready")
    logf_ready = sem("logf_ready")
    b_ready = sem("b_ready")
    lev_args, lev_exps, lev_ready = sem("lev_args"), sem("lev_exps"), sem("lev_ready")
    scores_done, at_ready, pv_done, o_copied = sem("scores_done"), sem("at_ready"), sem("pv_done"), sem("o_copied")
    kt_done, kt_copied, kv_done, state_ready = sem("kt_done"), sem("kt_copied"), sem("kv_done"), sem("state_ready")
    sq_ready, ssum_done, ssum_read, rstd_ready, o_normed = (
        sem("sq_ready"), sem("ssum_done"), sem("ssum_read"), sem("rstd_ready"), sem("o_normed"))
    gate_ready, silu_done, mixed_ready, mhi_ready, mlo_ready = (
        sem("gate_ready"), sem("silu_done"), sem("mixed_ready"), sem("mhi_ready"), sem("mlo_ready"))
    mix_stored = sem("mix_stored")
    mix_in = [sem(f"mix_in{i}") for i in range(NK - 2)]
    gatebc_in, lnwb_in = sem("gatebc_in"), sem("lnwb_in")
    xre_in = [sem(f"xre_in{i}") for i in range(4)]
    z_made = sem("z_made")
    z_scaled, z_normed, z_done, out_stored = sem("z_scaled"), sem("z_normed"), sem("z_done"), sem("out_stored")
    zrstd_ready, zvar_ready = sem("zrstd_ready"), sem("zvar_ready")

    block = ctx.enter_context(nc.Block())

    LAST_MIX = 4 * RET_HEADS + 2 * (HG_HEADS - 2)

    def in_step(panel, k):
        return panel * STEPS + (k + 1), k % RING, panel * 2 + (k // RING + 1)

    def out_step(blk, k):
        return blk * BSTEPS + (PANELS * STEPS + k + 1), k % RING, blk * 4 + (PANELS * 2 + k // RING + 1)

    def ret_chunk(r, c):
        return r * 8 + c

    def hg_chunk(n, c):
        return n * 8 + (8 * RET_HEADS + c)

    def ret_upd(r, c):
        return r * 7 + c

    def hg_upd(n, c):
        return n * 7 + (7 * RET_HEADS + c)

    def ret_norm(r, half):
        return r * 2 + half

    def hg_norm(n, half):
        return n * 2 + (2 * RET_HEADS + half)

    def ret_mix(r, half, e):
        return r * 4 + (2 * half + e)

    def hg_mix(n, half):
        return n * 2 + (4 * RET_HEADS + half)

    def quarters(row):
        return row.rearrange("p (a n) -> p a n", a=4)

    w_in_k = w_in[0].rearrange("(k p) n -> p k n", p=P)
    w_out_k = w_out[0].rearrange("(k p) n -> p k n", p=P)
    w_ada_k = w_ada[0].rearrange("(k p) n -> p k n", p=P)
    x_t = x[0].rearrange("(t p) n -> p t n", p=P)
    out_t = out[0].rearrange("(t p) n -> p t n", p=P)

    @block.sync
    def _(sp):
        sp.dma_start(ident[:], table_dram[:, 0:P]).then_inc(tables_in, 16)
        sp.dma_start(vecs[:, 82:84], table_dram[:, 9 * P + 8:9 * P + 10]).then_inc(tables_in, 16)
        sp.dma_start(vecs[:, 84:92], table_dram[:, 9 * P:9 * P + 8]).then_inc(tables_in, 16)
        sp.dma_start(pos_i[:], positions.to_broadcast([P, T])).then_inc(pos_in, 16)
        sp.wait_ge(set_up, 1)
        sp.dma_start(smalls[0:16, :], lb_logits.rearrange("a (h p) -> (a h) p", p=P)).then_inc(smalls_in, 16)
        sp.dma_start(smalls[16:24, :], hg_norm_w.rearrange("a (h p) -> (a h) p", p=P)).then_inc(smalls_in, 16)
        sp.dma_start(smalls[24:40, :], c.rearrange("a (k p) -> (a k) p", p=P)).then_inc(smalls_in, 16)
        sp.wait_ge(sums_zero, 1)
        sp.dma_start(ada_sum[0:1, :], b_ada[:, 0:2 * D]).then_inc(sums_in, 16)

        def ada(k):
            if k >= 3:
                sp.wait_ge(ada_used, k - 2)
            sp.dma_start(ada_in[k % 3][:], w_ada_k[:, k, 0:2 * D]).then_inc(ada_loaded[k % 3], 16)

        for t in range(NT):
            if t >= 2:
                sp.wait_ge(x_turned, 4 * (t - 1))
            sp.dma_start(x_in[t % 2][:], x_t[:, t, :]).then_inc(x_loaded[t % 2], 16)
            if t < 3:
                ada(t)
        sp.dma_start(masks[:], masks_dram).then_inc(tables_in, 16)
        for k in range(3, NK):
            ada(k)

        def slot_free(panel, k):
            if k >= RING:
                sp.wait_ge(w_used, panel * (STEPS - 1) + (k - RING + 1))
            elif k == RING - 1:
                sp.wait_ge(bank_done[3], panel)
            else:
                sp.wait_ge(w_used, panel * (STEPS - 1) + (k - RING + 2))

        def load_split(col, col2, kp):
            dst = w_raw[:, kp % RING, :].rearrange("p (k n) -> p k n", k=2)
            sp.dma_start(dst[:, :, 0:P], w_in_k[:, 2 * kp:2 * kp + 2, ds(col, P)]).then_inc(w_loaded[kp % RING], 16)
            sp.dma_start(dst[:, :, P:2 * P], w_in_k[:, 2 * kp:2 * kp + 2, ds(col2, P)]).then_inc(w_loaded[kp % RING], 16)

        def load_wide(col, kp):
            dst = w_raw[:, kp % RING, :].rearrange("p (k n) -> p k n", k=2)
            sp.dma_start(dst, w_in_k[:, 2 * kp:2 * kp + 2, ds(col, 2 * P)]).then_inc(w_loaded[kp % RING], 32)

        def panel_loads(panel, first, load):
            for kp in range(STEPS):
                if not first or kp >= RING:
                    slot_free(panel, kp)
                load(kp)

        def ret_loads(r, first=False):
            panel_loads(3 * r, first, lambda kp: load_split(C_RQ + P * r, C_RK + P * r, kp))
            panel_loads(3 * r + 1, False, lambda kp: load_wide(C_RV + 256 * r, kp))
            panel_loads(3 * r + 2, False, lambda kp: load_wide(C_RG + 256 * r, kp))

        ret_loads(0, True)
        with sp.Fori(1, RET_HEADS) as r:
            ret_loads(r)

        def hg_loads(p, last_behind=None):
            base = 4 * p + RET_PANELS
            panel_loads(base, False, lambda kp: load_split(C_HQ + 256 * p, C_HF + 256 * p, kp))
            panel_loads(base + 1, False, lambda kp: load_wide(C_HI + 256 * p, kp))
            panel_loads(base + 2, False, lambda kp: load_split(256 * p + (C_HQ + P), 256 * p + (C_HF + P), kp))
            panel_loads(base + 3, False, lambda kp: load_wide(C_HG + 256 * p, kp))

        with sp.Fori(0, PAIRS) as p:
            hg_loads(p)

        def out_slot_free(blk, k):
            if k >= RING:
                sp.wait_ge(w_used, blk * (BSTEPS - 1) + (PANELS * (STEPS - 1) + k - RING + 1))
            elif k == RING - 1:
                sp.wait_ge(bank_done[3], blk + PANELS)
            else:
                sp.wait_ge(w_used, blk * (BSTEPS - 1) + (PANELS * (STEPS - 1) + k - RING + 2))

        def load_out(blk, nb, k):
            sp.dma_start(w_raw[:, k % RING, :], w_out_k[:, k, ds(nb * 512, 512)]).then_inc(w_loaded[k % RING], 32)

        def load_mixed(m):
            sp.dma_start(h_hi[:, m, :].bitcast(F32), mix_hi_dram[m]).then_inc(mix_in[m], 16)
            sp.dma_start(h_lo[:, m, :].bitcast(F32), mix_lo_dram[m]).then_inc(mix_in[m], 16)

        last = PANELS - 1
        sp.wait_ge(mix_stored, 32 * 28)
        for k in range(RING):
            out_slot_free(0, k)
            load_out(0, 0, k)
            for kp in (k,) if k < 3 else (3, 4, 5, 6, 7):
                if kp < STEPS - 1:
                    sp.wait_ge(w_used, last * (STEPS - 1) + kp + 1)
                else:
                    sp.wait_ge(bank_done[3], PANELS)
                if kp < 7:
                    load_mixed(2 * kp)
                    load_mixed(2 * kp + 1)

        def out_loads(blk, nb, first_k=0):
            for k in range(first_k, BSTEPS):
                out_slot_free(blk, k)
                load_out(blk, nb, k)

        out_loads(0, 0, RING)
        with sp.Fori(1, 4) as nb:
            out_loads(nb, nb)
        with sp.Fori(0, 4) as nb:
            out_loads(nb + 4, nb)
        sp.wait_ge(out_stored, 16 * NT)
        sp.wait_ge(gate_stored, 16)

    @block.tensor
    def _(pe):
        def mm(*a, **k):
            return nc.tensor.matmul(*a, skip_group_check=True, **k)

        pe.wait_ge(tables_in, 48)
        pe.wait_ge(smalls_in, 48)
        nc.tensor.transpose(sc0[:, 0:P], smalls[:], ident[:]).then_inc(smalls_turned, 1)
        for t in range(NT):
            pe.wait_ge(x_normed, t + 1)
            for b in range(4):
                if t >= 1:
                    pe.wait_ge(x_placed, 4 * (t - 1) + b + 1)
                for j in range(4):
                    k = 4 * b + j
                    last = nc.tensor.transpose(main[:, b, j * P:(j + 1) * P], x_in[t % 2][:, k * P:(k + 1) * P], ident[:])
                last.then_inc(x_turned, 1)
        pe.wait_ge(ada_used, NK)
        for j in range(32):
            last = mm(sc1[:, j:j + 1], ada_sum[:, j * P:(j + 1) * P], ones[:, 0:1], start=(j == 0), stop=True)
        last.then_inc(mod_done, 1)

        parts = ((0, 0), (0, 1), (1, 0))
        w_part, h_part = (w_high, w_low), (h_hi, h_lo)

        def panel(pj, turned, hooks, first=False):
            for kp in range(STEPS):
                count, slot, _ = in_step(pj, kp)
                pe.wait_ge(w_lo_ready, count)
                if first:
                    pe.wait_ge(h_ready, 2 * kp + 2)
                for b in range(4):
                    if kp == 0 and first:
                        if b == 0:
                            pe.wait_ge(x_placed, 4 * NT)
                    elif kp == 0:
                        pe.wait_ge(bank_read[b], pj)
                    for kk in range(2):
                        k = 2 * kp + kk
                        if turned:
                            cc, half = b // 2, b % 2
                            for i, (wp, hp) in enumerate(parts):
                                last = mm(main[:, b, :], w_part[wp][:, slot, kk * 256 + cc * P:kk * 256 + (cc + 1) * P],
                                          h_part[hp][:, k, half * 512:(half + 1) * 512],
                                          start=(k == 0 and i == 0), stop=(k == NK - 1 and i == 2))
                        else:
                            for ti in range(2):
                                t = 2 * b + ti
                                for i, (hp, wp) in enumerate(parts):
                                    last = mm(main[:, b, ti * 256:(ti + 1) * 256], h_part[hp][:, k, t * P:(t + 1) * P],
                                              w_part[wp][:, slot, kk * 256:(kk + 1) * 256],
                                              start=(k == 0 and i == 0 and ti == 0), stop=(k == NK - 1 and i == 2))
                    if kp == STEPS - 1:
                        last.then_inc(bank_done[b], 1)
                    elif b == 3:
                        last.then_inc(w_used, 1)
                    for hook in hooks(kp, b):
                        hook()

        def ret_score(r, c):
            if c == 0:
                pe.wait_ge(rope_ready, r + 1)
            if not (isinstance(r, int) and r == 0 and c == 0):
                pe.wait_ge(at_ready, ret_chunk(r, c))
            cs = slice(c * P, (c + 1) * P)
            mm(sc0[:, 0:P], r_k[:, cs], r_q[:, cs], start=True, stop=True).then_inc(scores_done, 1)

        def ret_kt(r, c):
            cs = slice(c * P, (c + 1) * P)
            if c < 7:
                if not (isinstance(r, int) and r == 0 and c == 0):
                    pe.wait_ge(state_ready, ret_upd(r, c))
                if c == 0 and not isinstance(r, int):
                    pe.wait_ge(ssum_read, ret_norm(r, 0))
                if c == 0 and isinstance(r, int):
                    pe.wait_ge(gate_copied, 1)
                nc.tensor.transpose(aux[:, 0:P], r_k[:, cs], ident[:]).then_inc(kt_done, 1)

        def ret_apply(r, c):
            if c == 0:
                for b in range(4):
                    pe.wait_ge(bank_read[b], 3 * r + 2)
            pe.wait_ge(at_ready, ret_chunk(r, c + 1))
            if not (isinstance(r, int) and r == 0 and c == 0):
                pe.wait_ge(o_copied, ret_chunk(r, c))
            if c:
                pe.wait_ge(state_ready, ret_upd(r, c))
                pe.wait_ge(qx_ready, r + 1)
            for e in range(2):
                es = slice(e * P, (e + 1) * P)
                last = mm(ops[:, es], r_v[:, c, es], at_buf[:, c % 2, :], start=True, stop=(c == 0))
                if c:
                    last = mm(ops[:, es], state[:, es], r_qx[:, c * P:(c + 1) * P], start=False, stop=True)
            last.then_inc(pv_done, 1)
            if c < 7:
                pe.wait_ge(kt_copied, ret_upd(r, c + 1))
                mm(aux[:, P:P + RET_DV], kt_buf[:, c % 2, :], r_v[:, c, :], start=True, stop=True).then_inc(kv_done, 1)

        def ret_ssum(r, half):
            pe.wait_ge(sq_ready, ret_norm(r, half + 1))
            if half == 0:
                pe.wait_ge(state_ready, ret_upd(r, 7))
            else:
                pe.wait_ge(ssum_read, ret_norm(r, half))
            for e in range(2):
                last = mm(aux[:, :], ones[:], r_t[:, e * 512:(e + 1) * 512], start=(e == 0), stop=(e == 1))
            last.then_inc(ssum_done, 1)

        def hg_score(n, side, c):
            u, cc = c // 2, c % 2
            if cc == 0:
                pe.wait_ge(lev_ready, n * 4 + (u + 1))
            pe.wait_ge(at_ready, hg_chunk(n, c))
            for i in range(NL):
                g = lev[:, u % 2, i, cc * P:(cc + 1) * P]
                bank, col = (sc0, i * P) if i < 4 else (sc1, (i - 4) * P)
                mm(bank[:, col:col + P], g, g, start=True, stop=True)
            cs = slice(c * P, (c + 1) * P)
            mm(sc1[:, 3 * P:4 * P], g_k[:, cs], g_q[:, cs], start=True, stop=True).then_inc(scores_done, 1)

        def hg_kt(n, side, c):
            u, cc = c // 2, c % 2
            if c < 7:
                pe.wait_ge(state_ready, hg_upd(n, c))
                if c == 0 or (c == 4 and side):
                    pe.wait_ge(ssum_read, hg_norm(n, c // 4))
                nc.tensor.transpose(aux[:, 0:P], lev[:, u % 2, NL, cc * P:(cc + 1) * P], ident[:]).then_inc(kt_done, 1)

        def hg_apply(n, side, c):
            u, cc = c // 2, c % 2
            pe.wait_ge(at_ready, hg_chunk(n, c + 1))
            pe.wait_ge(o_copied, hg_chunk(n, c))
            v = g_v[:, c, side * P:(side + 1) * P]
            last = mm(ops[:, 0:P], v, at_buf[:, c % 2, :], start=True, stop=(c == 0))
            if c:
                pe.wait_ge(state_ready, hg_upd(n, c))
                last = mm(ops[:, 0:P], state[:, 0:P], qe[:, u % 2, cc * P:(cc + 1) * P], start=False, stop=True)
            last.then_inc(pv_done, 1)
            if c < 7:
                pe.wait_ge(kt_copied, hg_upd(n, c + 1))
                mm(aux[:, P:2 * P], kt_buf[:, c % 2, :], v, start=True, stop=True).then_inc(kv_done, 1)

        def hg_ssum(n, half, upd):
            pe.wait_ge(sq_ready, hg_norm(n, half + 1))
            pe.wait_ge(state_ready, upd)
            pe.wait_ge(ssum_read, hg_norm(n, half))
            mm(aux[:, :], ones[:], tmp_s[:], start=True, stop=True).then_inc(ssum_done, 1)

        def hg_hooks(n_a, n_b, w_a, w_b):
            def hooks(kp, b):
                todo = []
                for n, side, w0, score, apply in ((n_a, 0, w_a, A_SCORE, A_APPLY), (n_b, 1, w_b, B_SCORE, B_APPLY)):
                    if w0 is None:
                        continue
                    w = w0 + kp
                    if b == 0 and w in apply:
                        if side == 0 and apply[w] == 0:
                            todo.append(lambda n=n: v_in_place(n))
                        todo.append(lambda n=n, side=side, c=apply[w]: hg_apply(n, side, c))
                    if b == 1 and w in score:
                        todo.append(lambda n=n, side=side, c=score[w]: hg_score(n, side, c))
                    if b == 2 and w in score:
                        todo.append(lambda n=n, side=side, c=score[w]: hg_kt(n, side, c))
                if w_a is not None and b == 3 and w_a + kp in A_NORM:
                    todo.append(lambda half=A_NORM[w_a + kp]: hg_ssum(n_a, half, hg_upd(n_a, 7)))
                if w_b is not None and b == 3 and w_b + kp in B_NORM:
                    half = B_NORM[w_b + kp]
                    todo.append(lambda half=half: hg_ssum(n_b, half, hg_upd(n_b, 4 if half == 0 else 7)))
                return todo
            return hooks

        def v_in_place(n):
            for b in range(4):
                pe.wait_ge(bank_read[b], n * 2 + (RET_PANELS + 2))

        def no_hooks(kp, b):
            return ()

        def ret_hooks_g(r):
            def hooks(kp, b):
                if b == 0 and kp >= 1:
                    return (lambda: ret_apply(r, kp - 1),)
                if b == 1:
                    return (lambda: ret_score(r, kp),)
                if b == 2:
                    return (lambda: ret_kt(r, kp),)
                return ()
            return hooks

        def ret_hooks_after(r):
            def hooks(kp, b):
                if b == 0 and kp == 0:
                    return (lambda: ret_apply(r, 7),)
                if b == 2 and kp in (1, 2):
                    return (lambda: ret_ssum(r, kp - 1),)
                return ()
            return hooks

        def gate_sums(kp, b):
            if kp == 6 and b == 3:
                def work():
                    pe.wait_ge(gate_used, NK)
                    for j, bank in enumerate((sc0, sc1, ops, aux)):
                        last = mm(bank[:, :], ones[:], gate_sum[:, j * 512:(j + 1) * 512], start=True, stop=True)
                    last.then_inc(gate_turned, 1)
                return (work,)
            return ()

        panel(0, True, no_hooks, first=True)
        panel(1, False, gate_sums)
        panel(2, True, ret_hooks_g(0))
        with pe.Fori(1, RET_HEADS) as r:
            panel(3 * r, True, ret_hooks_after(r - 1))
            panel(3 * r + 1, False, no_hooks)
            panel(3 * r + 2, True, ret_hooks_g(r))

        def pair(p, before):
            base = 4 * p + RET_PANELS
            panel(base, True, before)
            panel(base + 1, False, hg_hooks(2 * p, None, 0, None))
            panel(base + 2, True, hg_hooks(2 * p, None, 8, None))
            panel(base + 3, True, hg_hooks(2 * p, 2 * p + 1, 16, 0))

        pair(0, ret_hooks_after(RET_HEADS - 1))
        with pe.Fori(1, PAIRS) as p:
            pair(p, hg_hooks(2 * p - 2, 2 * p - 1, 24, 8))

        def out_block(blk, half, hooks):
            for k in range(BSTEPS):
                count, slot, _ = out_step(blk, k)
                pe.wait_ge(w_lo_ready, count)
                if isinstance(blk, int) and blk == 0:
                    if k < NK - 2:
                        pe.wait_ge(mix_in[k], 32)
                    else:
                        pe.wait_ge(mlo_ready, LAST_MIX + (1, 3)[k - NK + 2])
                if isinstance(blk, int) and blk == 4 and k == 0:
                    pe.wait_ge(mlo_ready, LAST_MIX + 4)
                for b in range(4):
                    if k == 0:
                        pe.wait_ge(bank_read[b], blk + PANELS)
                    t = half * 4 + b
                    for i, (hp, wp) in enumerate(parts):
                        last = mm(main[:, b, :], h_part[hp][:, k, t * P:(t + 1) * P], w_part[wp][:, slot, :],
                                  start=(k == 0 and i == 0), stop=(k == BSTEPS - 1 and i == 2))
                    if k == BSTEPS - 1:
                        last.then_inc(bank_done[b], 1)
                    elif b == 3:
                        last.then_inc(w_used, 1)
                    for hook in hooks(k // 2, 2 * (k % 2) + b // 2) if b % 2 == 1 else ():
                        hook()

        out_block(0, 0, hg_hooks(HG_HEADS - 2, HG_HEADS - 1, 24, 8))
        with pe.Fori(1, 4) as nb:
            out_block(nb, 0, no_hooks)
        out_block(4, 1, no_hooks)
        with pe.Fori(5, 8) as blk:
            out_block(blk, 1, no_hooks)

    @block.scalar
    def _(act):
        fn = nc.scalar.activation

        nc.scalar.preload_act_table_set("natural_log_exp_and_others")
        act.wait_ge(smalls_turned, 1)
        fn(smalls_t[:], sc0[:, 0:40], ACT.Copy).then_inc(smalls_placed, 1)
        act.wait_ge(smalls_placed, 1)
        fn(cond, smalls_t[:, 24:40], ACT.Exp, scale=-1.0).then_inc(cond_exp, 1)
        act.wait_ge(lb_diff, 1)
        fn(lbtmp, lbtmp, ACT.Exp).then_inc(lb_exp, 1)
        act.wait_ge(lb_ready, 1)
        fn(ln_upper, ln_upper, ACT.Ln).then_inc(ln_ready, 1)
        for t in range(NT):
            act.wait_ge(x_stats, t + 1)
            m, v = stats[:, 2 * t:2 * t + 1], stats[:, 2 * t + 1:2 * t + 2]
            fn(v, v, ACT.Ln, bias=eps_t)
            act.drain()
            fn(v, v, ACT.Exp, scale=-0.5)
            act.drain()
            fn(m, m, ACT.Copy, scale=v)
            act.drain()
            fn(m, m, ACT.Copy, scale=-1.0)
            act.drain()
            fn(x_in[t % 2][:], x_in[t % 2][:], ACT.Identity, bias=m, scale=v).then_inc(x_normed, 1)
            for b in range(4):
                act.wait_ge(x_turned, 4 * t + b + 1)
                fn(lnx_t[:, 4 * b:4 * b + 4, t * P:(t + 1) * P],
                   main[:, b, :].rearrange("p (k n) -> p k n", k=4), ACT.Copy).then_inc(x_placed, 1)
        act.wait_ge(angle_ready, 1)
        fn(cos_t[:], turns[:], ACT.Sin, bias=half_pi, scale=-1.0)
        fn(sin_t[:], angle[:], ACT.Sin)
        act.drain()
        fn(sin_t[:], sin_t[:], ACT.Copy, scale=sign_t).then_inc(trig_ready, 1)
        nc.scalar.preload_act_table_set("natural_log_exp_and_others")

        def w_hi(step):
            count, slot, use = step
            act.wait_ge(w_loaded[slot], use * 32)
            fn(w_high[:, slot, :], w_raw[:, slot, :], ACT.Copy).then_inc(w_hi_ready, 1)

        def lead(pj, k):
            w_hi(in_step(pj, k + LEAD) if k + LEAD < STEPS else in_step(pj + 1, k + LEAD - STEPS))

        for k in range(LEAD):
            w_hi(in_step(0, k))
        act.wait_ge(mod_ready, 1)
        act.wait_ge(ada_used, NK)
        act.wait_ge(x_turned, 4 * NT)
        act.drain()
        for k in range(NK):
            if k >= 2:
                act.wait_ge(h_ready, k - 1)
            fn(h_tmp[:, k % 2, :], lnx_t[:, k, :], ACT.Identity, bias=shift_t[:, k:k + 1],
                        scale=scale1_t[:, k:k + 1])
            act.drain()
            fn(h_hi[:, k, :], h_tmp[:, k % 2, :], ACT.Copy).then_inc(h_made, 1)
            if k % 2:
                lead(0, k // 2)

        def read_banks(pj, dsts, banks):
            for b, dst in zip(banks, dsts):
                act.wait_ge(bank_done[b], pj + 1)
                fn(dst, main[:, b, :], ACT.Copy).then_inc(bank_read[b], 1)

        def ret_read_qk(r, pj):
            if isinstance(r, int):
                act.wait_ge(h_ready, NK)
            else:
                act.wait_ge(pv_done, ret_chunk(r, 0))
            read_banks(pj, (r_k[:, 0:512], r_k[:, 512:T]), (2, 3))

        def ret_read_v(r, pj):
            if isinstance(r, int):
                act.wait_ge(gate_stored, 16)
            else:
                act.wait_ge(pv_done, ret_chunk(r, 0))
            read_banks(pj, (r_v[:, 4:6, :], r_v[:, 6:8, :]), (2, 3))

        def ret_read_g(r, pj):
            if not isinstance(r, int):
                act.wait_ge(mixed_ready, ret_mix(r, 0, 0))
            read_banks(pj, (r_g[:, 1, 0:512], r_g[:, 1, 512:T]), (2, 3))

        def copy_kt(update, c, scale):
            act.wait_ge(kt_done, update + 1)
            fn(kt_buf[:, c % 2, :], aux[:, 0:P], ACT.Copy, scale=scale).then_inc(kt_copied, 1)

        def ret_chunk_work(r, c_score, c_apply):
            if c_apply is not None:
                act.wait_ge(pv_done, ret_chunk(r, c_apply + 1))
                if c_apply == 0 and not isinstance(r, int):
                    act.wait_ge(mix_stored, ret_mix(r, 0, 0) * 32)
                fn(r_o[:, :, c_apply * P:(c_apply + 1) * P], ops[:, 0:256].rearrange("p (e n) -> p e n", e=2),
                   ACT.Copy).then_inc(o_copied, 1)
            if c_score is not None and c_score < 7:
                copy_kt(ret_upd(r, c_score), c_score, head_vecs[:, 0:1])

        def hg_chunk_work(n, side, c_score, c_apply, o_free=None):
            if c_apply is not None:
                act.wait_ge(pv_done, hg_chunk(n, c_apply + 1))
                if c_apply == 0:
                    act.wait_ge(mix_stored, o_free)
                fn(g_o[:, side, c_apply * P:(c_apply + 1) * P], ops[:, 0:P], ACT.Copy).then_inc(o_copied, 1)
            if c_score is not None and c_score < 7:
                copy_kt(hg_upd(n, c_score), c_score, 1.0)

        def rstd(norm, width):
            act.wait_ge(ssum_done, norm + 1)
            act.wait_ge(o_normed, norm)
            fn(tmp_e[:], aux[:, :], ACT.Ln, scale=1.0 / width, bias=eps_t).then_inc(ssum_read, 1)
            act.wait_ge(ssum_read, norm + 1)
            fn(tmp_e[:], tmp_e[:], ACT.Exp, scale=-0.5).then_inc(rstd_ready, 1)

        def gate_sigmoid(mix, norm, gates):
            act.wait_ge(o_normed, norm)
            act.wait_ge(silu_done, mix) if not (isinstance(mix, int) and mix == 0) else None
            fn(tmp_e[:], gates, ACT.Exp, scale=-1.0)
            act.drain()
            fn(tmp_e[:], tmp_e[:], ACT.Ln, bias=one_t)
            act.drain()
            fn(tmp_e[:], tmp_e[:], ACT.Exp, scale=-1.0).then_inc(gate_ready, 1)

        def mixed_hi(mix, norm, o):
            act.wait_ge(mixed_ready, mix + 1)
            act.wait_ge(ssum_done, norm)
            if not (isinstance(mix, int) and mix == 0):
                act.wait_ge(mix_stored, mix * 32)
            fn(tmp_hi[:], o, ACT.Copy).then_inc(mhi_ready, 1)

        def ret_after(r, kp):
            if kp in (1, 2):
                rstd_guard(r, kp - 1)
            if kp in (3, 4, 5, 6):
                i = kp - 3
                half, e = i // 2, i % 2
                hs = slice(half * 512, (half + 1) * 512)
                gate_sigmoid(ret_mix(r, half, e), ret_norm(r, 2), r_g[:, e, hs])
                mixed_hi(ret_mix(r, half, e), ret_norm(r, 2), r_o[:, e, hs])

        def rstd_guard(r, half):
            norm = ret_norm(r, half)
            act.wait_ge(ssum_done, norm + 1)
            if not (isinstance(r, int) and r == 0 and half == 0):
                act.wait_ge(o_normed, norm)
            if not (isinstance(r, int) and r == 0) and half == 0:
                act.wait_ge(silu_done, ret_mix(r, 0, 0))
            fn(tmp_e[:], aux[:, :], ACT.Ln, scale=1.0 / RET_DV, bias=eps_t).then_inc(ssum_read, 1)
            act.wait_ge(ssum_read, norm + 1)
            fn(tmp_e[:], tmp_e[:], ACT.Exp, scale=-0.5).then_inc(rstd_ready, 1)

        def ret_head(r, first):
            if first:
                pass
            else:
                for kp in range(STEPS):
                    if kp == 0:
                        ret_read_g(r - 1, 3 * r - 1)
                    if kp == 0:
                        ret_chunk_work(r - 1, None, 7)
                    lead(3 * r, kp)
                    ret_after(r - 1, kp)
            for kp in range(STEPS):
                if kp == 0:
                    ret_read_qk(r, 3 * r)
                lead(3 * r + 1, kp)
                if first and kp == 7:
                    act.wait_ge(gate_turned, 1)
                    for j, bank in enumerate((sc0, sc1, ops, aux)):
                        last = fn(gate_out[0:1, j * 512:(j + 1) * 512], bank[0:1, :], ACT.Copy)
                    last.then_inc(gate_copied, 1)
            for kp in range(STEPS):
                if kp == 0:
                    ret_read_v(r, 3 * r + 1)
                ret_chunk_work(r, kp, kp - 1 if kp else None)
                lead(3 * r + 2, kp)

        ret_head(0, True)
        with act.Fori(1, RET_HEADS) as r:
            nc.scalar.preload_act_table_set("natural_log_exp_and_others")
            ret_head(r, False)

        def hg_read_qf(n, pj, first=False):
            if first:
                act.wait_ge(mix_stored, 32 * 16)
                act.wait_ge(pv_done, 8 * RET_HEADS)
            else:
                act.wait_ge(lev_ready, n * 4)
                act.wait_ge(scores_done, hg_chunk(n, 0))
            for b in (2, 3):
                hs = slice((b - 2) * 512, (b - 1) * 512)
                act.wait_ge(bank_done[b], pj + 1)
                fn(g_b[:, hs], main[:, b, :], ACT.Exp, scale=-1.0)
                fn(g_k[:, hs], main[:, b, :], ACT.Exp).then_inc(bank_read[b], 1)
            act.drain()
            fn(g_b[:], g_b[:], ACT.Ln, bias=one_t)
            fn(g_k[:], g_k[:], ACT.Ln, bias=one_t)

        def hg_log(n):
            act.drain()
            fn(g_b[:], g_b[:], ACT.Exp, scale=-1.0)
            act.wait_ge(head_ready, n + 1)
            fn(g_k[:], g_k[:], ACT.Exp, scale=-1.0, bias=head_vecs[:, 3:4])
            act.drain()
            fn(g_b[:], g_b[:], ACT.Ln, scale=head_vecs[:, 1:2], bias=head_vecs[:, 2:3]).then_inc(logf_ready, 1)

        def hg_exps(n, u):
            buf = u % 2
            us = slice(u * 256, (u + 1) * 256)
            if u == 0:
                act.wait_ge(b_ready, n + 1)
            act.wait_ge(lev_args, n * 4 + (u + 1))
            fn(dec_t[:, buf, :], g_b[:, us].rearrange("p (c n) -> p c n", n=P)[:, :, P - 1], ACT.Exp)
            fn(qe[:, buf, :], g_b[:, us], ACT.Exp)
            fn(lev[:, buf, :, :], lev[:, buf, :, :], ACT.Exp).then_inc(lev_exps, 1)

        def hg_chunks(n, side, w, score, apply, o_free):
            c_s, c_a = score.get(w), apply.get(w)
            if c_s is not None or c_a is not None:
                hg_chunk_work(n, side, c_s, c_a, o_free)

        def hg_window(n, w, gen, norm):
            if w == 1:
                hg_log(n)
            if w in norm:
                rstd_hg(n, norm[w])
            for u, at_ in gen.items():
                if at_ == w:
                    hg_exps(n, u)

        def rstd_hg(n, half):
            rstd(hg_norm(n, half), P)

        def hg_mix_work(n, side, half, norm, tail=False):
            hs = slice(half * 512, (half + 1) * 512)
            mix = hg_mix(n, half)
            gate_sigmoid(mix, norm, g_g[:, side, hs])
            if tail:
                act.wait_ge(mixed_ready, mix + 1)
                act.wait_ge(bank_done[3], PANELS)
                fn(h_hi[:, NK - 2 + side, hs], g_o[:, side, hs], ACT.Copy).then_inc(mhi_ready, 1)
            else:
                mixed_hi(mix, norm, g_o[:, side, hs])

        def tail_window(n_a, n_b, w, tail):
            hg_window(n_b, w, B_GEN, B_NORM)
            if w + 16 in A_MIX:
                hg_mix_work(n_a, 0, A_MIX[w + 16], hg_norm(n_b, 1), tail)
            if w in B_MIX:
                hg_mix_work(n_b, 1, B_MIX[w], hg_norm(n_b, B_NORM_DONE[w]), tail)

        B_NORM_DONE = {11: 1, 14: 2}

        def hg_read_g(pj):
            read_banks(pj, (g_g[:, 1, 0:512], g_g[:, 1, 512:T]), (2, 3))

        def pair(p, first):
            base = 4 * p + RET_PANELS
            for kp in range(STEPS):
                if kp == 0:
                    if first:
                        ret_read_g(RET_HEADS - 1, base - 1)
                    else:
                        hg_read_g(base - 1)
                if first:
                    if kp == 0:
                        ret_chunk_work(RET_HEADS - 1, None, 7)
                else:
                    hg_chunks(2 * p - 1, 1, 8 + kp, B_SCORE, B_APPLY, 0)
                lead(base, kp)
                if first:
                    ret_after(RET_HEADS - 1, kp)
                else:
                    tail_window(2 * p - 2, 2 * p - 1, 8 + kp, False)
            o_free = p * 128 + 32 * 16
            for kp in range(STEPS):
                if kp == 0:
                    hg_read_qf(2 * p, base, first)
                lead(base + 1, kp)
                hg_window(2 * p, kp, A_GEN, {})
            for kp in range(STEPS):
                if kp == 0:
                    read_banks(base + 1, (g_v[:, 4:6, :], g_v[:, 6:8, :]), (2, 3))
                hg_chunks(2 * p, 0, 8 + kp, A_SCORE, A_APPLY, o_free)
                lead(base + 2, kp)
                hg_window(2 * p, 8 + kp, A_GEN, {})
            for kp in range(STEPS):
                if kp == 0:
                    hg_read_qf(2 * p + 1, base + 2)
                hg_chunks(2 * p, 0, 16 + kp, A_SCORE, A_APPLY, o_free)
                hg_chunks(2 * p + 1, 1, kp, B_SCORE, B_APPLY, o_free)
                lead(base + 3, kp)
                hg_window(2 * p, 16 + kp, {}, A_NORM)
                hg_window(2 * p + 1, kp, B_GEN, {})

        pair(0, True)
        with act.Fori(1, PAIRS) as p:
            nc.scalar.preload_act_table_set("natural_log_exp_and_others")
            pair(p, False)

        def out_lead(blk, k, last=False):
            k2 = k + LEAD
            if k2 < BSTEPS:
                w_hi(out_step(blk, k2))
            elif not last:
                w_hi(out_step(blk + 1, k2 - BSTEPS))

        hg_read_g(PANELS - 1)
        for k in range(BSTEPS):
            if k % 2:
                hg_chunks(HG_HEADS - 1, 1, 8 + k // 2, B_SCORE, B_APPLY, 0)
            out_lead(0, k)
            if k % 2:
                tail_window(HG_HEADS - 2, HG_HEADS - 1, 8 + k // 2, True)
        with act.Fori(1, 4) as nb:
            for k in range(BSTEPS):
                out_lead(nb, k)

        def z_rstd(i):
            act.wait_ge(zvar_ready, i + 1)
            v = stats[:, 32 + 2 * (i % 4) + 1:32 + 2 * (i % 4) + 2]
            fn(v, v, ACT.Ln, bias=eps_t)
            act.drain()
            fn(v, v, ACT.Exp, scale=-0.5).then_inc(zrstd_ready, 1)

        for k in range(BSTEPS):
            out_lead(4, k)
            if k < 4:
                z_rstd(k)
        with act.Fori(5, 7) as blk:
            for k in range(BSTEPS):
                out_lead(blk, k)
        for k in range(BSTEPS):
            out_lead(7, k, True)
        for i in range(4, 8):
            z_rstd(i)

    @block.vector
    def _(dve):
        tt, ts, stt = nc.vector.tensor_tensor, nc.vector.tensor_scalar, nc.vector.scalar_tensor_tensor

        nc.vector.memset(ada_sum[:], 0.0)
        dve.drain()
        nc.vector.memset(lbtmp, 0.0).then_inc(sums_zero, 1)
        dve.wait_ge(pos_in, 16)
        dve.wait_ge(tables_in, 48)
        nc.vector.tensor_copy(turns[:], pos_i[:])
        dve.drain()
        ts(angle[:], turns[:], freq_t, None, ALU.mult)
        dve.drain()
        big = 12582912.0
        ts(turns[:], angle[:], float(1.0 / (2.0 * np.pi)), big, ALU.mult, ALU.add)
        dve.drain()
        ts(turns[:], turns[:], big, None, ALU.subtract)
        dve.drain()
        rest = 2.0 * np.pi
        for unit in (2.0 ** -5, 2.0 ** -13, 2.0 ** -21, None):
            part = float(np.floor(rest / unit) * unit) if unit else float(np.float32(rest))
            rest -= part
            stt(out=angle[:], in0=turns[:], scalar=-part, in1=angle[:], op0=ALU.mult, op1=ALU.add)
            dve.drain()
        ts(angle[:], angle[:], 3.1415925, -3.1415925, ALU.min, ALU.max)
        dve.drain()
        stt(out=turns[:], in0=angle[:], scalar=-1.0, in1=angle[:], op0=ALU.mult, op1=ALU.max).then_inc(angle_ready, 1)

        dve.wait_ge(smalls_placed, 1)
        l0, l1 = smalls_t[:, 0:8], smalls_t[:, 8:16]
        tt(lower, l0, l1, ALU.max)
        dve.drain()
        tt(lbtmp[:, 0:8], l0, lower, ALU.subtract)
        tt(lbtmp[:, 8:16], l1, lower, ALU.subtract)
        dve.drain()
        nc.vector.memset(half_pi, float(np.pi / 2)).then_inc(lb_diff, 1)
        dve.wait_ge(cond_exp, 1)
        ts(cond, cond, 1.0, None, ALU.add)
        dve.drain()
        nc.vector.reciprocal(cond, cond)
        dve.drain()
        tt(cond, cond, smalls_t[:, 24:40], ALU.mult).then_inc(cond_ready, 1)
        dve.wait_ge(lb_exp, 1)
        tt(lower, lbtmp[:, 0:8], lbtmp[:, 8:16], ALU.add)
        dve.drain()
        nc.vector.reciprocal(upper, lower)
        dve.drain()
        tt(lower, lbtmp[:, 0:8], upper, ALU.mult)
        dve.drain()
        ts(upper, lower, -1.0, 1.0, ALU.mult, ALU.add)
        dve.drain()
        ts(ln_upper, upper, 2.0 ** -60, None, ALU.max)
        ts(lower, lower, 2.0 ** -60, None, ALU.max).then_inc(lb_ready, 1)
        dve.wait_ge(cond_ready, 1)
        dve.wait_ge(sums_in, 16)

        def ada_add(k):
            dve.wait_ge(ada_loaded[k % 3], 16 * (k // 3 + 1))
            if k:
                dve.wait_ge(ada_used, k)
            stt(out=ada_sum[:], in0=ada_in[k % 3][:], scalar=cond[:, k:k + 1], in1=ada_sum[:],
                op0=ALU.mult, op1=ALU.add).then_inc(ada_used, 1)

        for t in range(NT):
            dve.drain()
            dve.wait_ge(x_loaded[t % 2], 16 * (t // 2 + 1))
            for j in range(4):
                nc.vector.bn_stats(stats[:, 32 + 6 * j:38 + 6 * j], x_in[t % 2][:, j * 512:(j + 1) * 512])
            dve.drain()
            nc.vector.bn_aggr(stats[:, 2 * t:2 * t + 2], stats[:, 32:56]).then_inc(x_stats, 1)
            if t < 3:
                ada_add(t)
        for k in range(3, NK):
            ada_add(k)
        dve.wait_ge(mod_done, 1)
        nc.vector.tensor_copy(shift_t, sc1[:, 0:16])
        ts(scale1_t, sc1[:, 16:32], 1.0, None, ALU.add)
        dve.drain()
        nc.vector.memset(gate_sum[:], 0.0)
        dve.drain()
        nc.vector.memset(dec_t[:], 0.0).then_inc(mod_ready, 1)
        nc.vector.memset(stats[:, 56:64], 0.0).then_inc(sums_zero, 1)

        def w_lo(step):
            count, slot, _ = step
            dve.wait_ge(w_hi_ready, count)
            tt(w_low[:, slot, :], w_raw[:, slot, :], w_high[:, slot, :].bitcast(F32), ALU.subtract).then_inc(w_lo_ready, 1)

        def lead(pj, k):
            w_lo(in_step(pj, k + LEAD) if k + LEAD < STEPS else in_step(pj + 1, k + LEAD - STEPS))

        for k in range(LEAD):
            w_lo(in_step(0, k))
        for k in range(NK):
            dve.wait_ge(h_made, k + 1)
            tt(h_lo[:, k, :], h_tmp[:, k % 2, :], h_hi[:, k, :].bitcast(F32), ALU.subtract).then_inc(h_ready, 1)
            if k % 2:
                lead(0, k // 2)
            dve.wait_ge(gate_loaded[k % 2], 16 * (k // 2 + 1))
            if k == 0:
                dve.wait_ge(gate_bias_in, 16)
            else:
                dve.wait_ge(gate_used, k)
            stt(out=gate_sum[:], in0=gate_in[k % 2][:], scalar=cond[:, k:k + 1], in1=gate_sum[:],
                op0=ALU.mult, op1=ALU.add).then_inc(gate_used, 1)

        def read_banks(pj, dsts, banks):
            for b, dst in zip(banks, dsts):
                dve.wait_ge(bank_done[b], pj + 1)
                nc.vector.tensor_copy(dst, main[:, b, :]).then_inc(bank_read[b], 1)

        def rope(x_, pj, banks):
            for b in banks:
                dve.wait_ge(bank_read[b], pj + 1)
            tt(r_t[0:64, :], x_[64:P, :], sin_t[64:P, :], ALU.mult)
            tt(r_t[64:P, :], x_[0:64, :], sin_t[0:64, :], ALU.mult)
            dve.drain()
            tt(x_[:], x_[:], cos_t[:], ALU.mult)
            dve.drain()

        def ret_rope(r, pj):
            dve.wait_ge(trig_ready, 1)
            ts(head_vecs[:, 0:1], k_decay[:, ds(r, 1)], 1.0, None, ALU.mult)
            if not isinstance(r, int):
                dve.wait_ge(ssum_done, ret_norm(r, 0))
            rope(r_q, pj, (0, 1))
            tt(r_q[:], r_q[:], r_t[:], ALU.add)
            dve.drain()
            rope(r_k, pj, (2, 3))
            tt(r_k[:], r_k[:], r_t[:], ALU.add).then_inc(rope_ready, 1)

        def ret_select(r, c):
            dve.wait_ge(scores_done, ret_chunk(r, c + 1))
            if not (isinstance(r, int) and r == 0 and c < 2):
                dve.wait_ge(pv_done, ret_chunk(r, c - 1))
            if isinstance(r, int) and c == 0:
                dve.wait_ge(decay_in, 32)
            tt(at_buf[:, c % 2, :], sc0[:, 0:P], decay_m[:, ds(r, 1), :].rearrange("p a n -> p (a n)"),
               ALU.mult).then_inc(at_ready, 1)

        def ret_update(r, c):
            dve.wait_ge(kv_done, ret_upd(r, c + 1))
            if c == 0:
                nc.vector.tensor_copy(state[:], aux[:, P:P + RET_DV]).then_inc(state_ready, 1)
            else:
                dve.wait_ge(state_ready, ret_upd(r, c))
                stt(out=state[:], in0=state[:], scalar=chunk_decay[:, ds(r, 1)], in1=aux[:, P:P + RET_DV],
                    op0=ALU.mult, op1=ALU.add).then_inc(state_ready, 1)

        def silu_mul(mix, gates, o, weight):
            dve.wait_ge(gate_ready, mix + 1)
            tt(gates, gates, tmp_e[:], ALU.mult).then_inc(silu_done, 1)
            dve.wait_ge(silu_done, mix + 1)
            if weight is None:
                tt(o, o, gates, ALU.mult).then_inc(mixed_ready, 1)
            else:
                stt(out=o, in0=o, scalar=weight, in1=gates, op0=ALU.mult, op1=ALU.mult).then_inc(mixed_ready, 1)

        def mixed_lo_in_place(mix, side, hs):
            dve.wait_ge(mhi_ready, mix + 1)
            tt(h_lo[:, NK - 2 + side, hs], g_o[:, side, hs], h_hi[:, NK - 2 + side, hs].bitcast(F32),
               ALU.subtract).then_inc(mlo_ready, 1)

        def mixed_lo(mix, o):
            dve.wait_ge(mhi_ready, mix + 1)
            tt(o, o, tmp_hi[:].bitcast(F32), ALU.subtract).then_inc(mlo_ready, 1)

        def ret_after(r, kp):
            if kp in (1, 2):
                half = kp - 1
                hs = slice(half * 512, (half + 1) * 512)
                dve.wait_ge(rstd_ready, ret_norm(r, half + 1))
                tt(r_o[:, 0, hs], r_o[:, 0, hs], tmp_e[:], ALU.mult)
                tt(r_o[:, 1, hs], r_o[:, 1, hs], tmp_e[:], ALU.mult).then_inc(o_normed, 1)
            if kp in (3, 4, 5, 6):
                half, e = (kp - 3) // 2, (kp - 3) % 2
                hs = slice(half * 512, (half + 1) * 512)
                if kp == 3:
                    dve.drain()
                    dve.wait_ge(o_normed, ret_norm(r, 2))
                mix = ret_mix(r, half, e)
                silu_mul(mix, r_g[:, e, hs], r_o[:, e, hs], None)
                mixed_lo(mix, r_o[:, e, hs])

        def ret_read_g(r, pj):
            if not (isinstance(r, int) and r == 0):
                dve.wait_ge(mixed_ready, ret_mix(r, 0, 0))
            read_banks(pj, (r_g[:, 0, 0:512], r_g[:, 0, 512:T]), (0, 1))

        def ret_head(r, first):
            if not first:
                for kp in range(STEPS):
                    if kp == 0:
                        ret_read_g(r - 1, 3 * r - 1)
                    lead(3 * r, kp)
                    ret_after(r - 1, kp)
            for kp in range(STEPS):
                if kp == 0:
                    if not first:
                        dve.wait_ge(pv_done, ret_chunk(r, 0))
                    read_banks(3 * r, (r_q[:, 0:512], r_q[:, 512:T]), (0, 1))
                lead(3 * r + 1, kp)
                if kp == 1:
                    ret_rope(r, 3 * r)
            for kp in range(STEPS):
                if kp == 0:
                    if first:
                        dve.wait_ge(gate_stored, 16)
                    else:
                        dve.wait_ge(pv_done, ret_chunk(r, 0))
                    read_banks(3 * r + 1, (r_v[:, 0:2, :], r_v[:, 2:4, :]), (0, 1))
                if kp:
                    ret_update(r, kp - 1)
                ret_select(r, kp)
                lead(3 * r + 2, kp)

        dve.wait_ge(tables_in, 64)
        ret_head(0, True)
        with dve.Fori(1, RET_HEADS) as r:
            ret_head(r, False)

        def hg_read_q(n, pj, first=False):
            if first:
                dve.wait_ge(mix_stored, 32 * 16)
                dve.wait_ge(pv_done, 8 * RET_HEADS)
                dve.wait_ge(ln_ready, 1)
            else:
                dve.wait_ge(lev_ready, n * 4)
                dve.wait_ge(scores_done, hg_chunk(n, 0))
            hg_head(n)
            read_banks(pj, (g_q[:, 0:512], g_q[:, 512:T]), (0, 1))

        def hg_head(n):
            ts(head_vecs[:, 1:2], upper[:, ds(n, 1)], 1.0, None, ALU.mult)
            ts(head_vecs[:, 2:3], lower[:, ds(n, 1)], 1.0, None, ALU.mult)
            ts(head_vecs[:, 3:4], ln_upper[:, ds(n, 1)], 1.0, None, ALU.mult).then_inc(head_ready, 1)

        def hg_cumsum(n):
            dve.wait_ge(logf_ready, n + 1)
            for c in range(8):
                cs = slice(c * P, (c + 1) * P)
                last = nc.vector.tensor_tensor_scan(g_b[:, cs], ones[:], g_b[:, cs], 0.0, ALU.mult, ALU.add)
            last.then_inc(b_ready, 1)

        def hg_args(n, u, first=False):
            buf = u % 2
            b = g_b[:, u * 256:(u + 1) * 256]
            if u == 0:
                dve.wait_ge(b_ready, n + 1)
            if not (first and u < 2):
                dve.wait_ge(pv_done, hg_chunk(n, 2 * (u - 1)))
            for i, m in enumerate(LEVELS):
                bv = b.rearrange("p (n h m) -> p n h m", h=2, m=m)
                lv = lev[:, buf, i, :].rearrange("p (n h m) -> p n h m", h=2, m=m)
                mid = bv[:, :, 0, m - 1:m].to_broadcast([P, P // m, m])
                tt(lv[:, :, 0, :], mid, bv[:, :, 0, :], ALU.subtract)
                tt(lv[:, :, 1, :], bv[:, :, 1, :], mid, ALU.subtract)
            bv = b.rearrange("p (c m) -> p c m", m=P)
            tt(lev[:, buf, NL, :].rearrange("p (c m) -> p c m", m=P), bv[:, :, P - 1:P].to_broadcast([P, 2, P]), bv,
               ALU.subtract).then_inc(lev_args, 1)

        def hg_select(n, c):
            dve.wait_ge(scores_done, hg_chunk(n, c + 1))
            dve.wait_ge(pv_done, hg_chunk(n, c - 1))
            a = at_buf[:, c % 2, :]
            tt(a, sc1[:, 3 * P:4 * P], ident[:], ALU.mult)
            dve.drain()
            nc.vector.tensor_copy(a[0:64, 64:P], sc0[0:64, 64:P])
            for i in range(1, NL):
                dve.drain()
                bank, col = (sc0, i * P) if i < 4 else (sc1, (i - 4) * P)
                last = nc.vector.copy_predicated(a, masks[:, (i - 1) * P:i * P], bank[:, col:col + P])
            last.then_inc(at_ready, 1)

        def hg_update(n, c):
            dve.wait_ge(kv_done, hg_upd(n, c + 1))
            if c == 0:
                nc.vector.tensor_copy(state[:, 0:P], aux[:, P:2 * P]).then_inc(state_ready, 1)
            else:
                dve.wait_ge(state_ready, hg_upd(n, c))
                stt(out=state[:, 0:P], in0=state[:, 0:P], scalar=dec_t[:, (c // 2) % 2, c % 2:c % 2 + 1],
                    in1=aux[:, P:2 * P], op0=ALU.mult, op1=ALU.add).then_inc(state_ready, 1)

        def hg_scale_o(n, side, half):
            hs = slice(half * 512, (half + 1) * 512)
            dve.wait_ge(rstd_ready, hg_norm(n, half + 1))
            tt(g_o[:, side, hs], g_o[:, side, hs], tmp_e[:], ALU.mult).then_inc(o_normed, 1)

        def hg_chunks(n, w, score, apply):
            if w in apply and apply[w] < 7:
                hg_update(n, apply[w])
            if w in score:
                hg_select(n, score[w])

        def hg_window(n, side, w, gen, norm, first=False):
            if w == 1:
                hg_cumsum(n)
            if w in norm:
                hg_scale_o(n, side, norm[w])
            for u, at_ in gen.items():
                if at_ == w:
                    hg_args(n, u, first)

        def hg_mix_work(n, side, half, tail):
            hs = slice(half * 512, (half + 1) * 512)
            mix = hg_mix(n, half)
            dve.wait_ge(o_normed, hg_norm(n, half + 1))
            silu_mul(mix, g_g[:, side, hs], g_o[:, side, hs], smalls_t[:, ds(16 + n, 1)])
            if tail:
                mixed_lo_in_place(mix, side, hs)
            else:
                mixed_lo(mix, g_o[:, side, hs])

        def tail_window(n_a, n_b, w, tail=False):
            hg_window(n_b, 1, w, B_GEN, B_NORM)
            if w + 16 in A_MIX:
                hg_mix_work(n_a, 0, A_MIX[w + 16], tail)
            if w in B_MIX:
                hg_mix_work(n_b, 1, B_MIX[w], tail)

        def hg_read_g(pj, n):
            if not isinstance(n, int) or n:
                dve.wait_ge(mixed_ready, hg_mix(n, 0))
            read_banks(pj, (g_g[:, 0, 0:512], g_g[:, 0, 512:T]), (0, 1))

        def pair(p, first):
            base = 4 * p + RET_PANELS
            for kp in range(STEPS):
                if kp == 0:
                    if first:
                        ret_read_g(RET_HEADS - 1, base - 1)
                    else:
                        hg_read_g(base - 1, 2 * p - 2)
                if not first:
                    hg_chunks(2 * p - 1, 8 + kp, B_SCORE, B_APPLY)
                lead(base, kp)
                if first:
                    ret_after(RET_HEADS - 1, kp)
                else:
                    tail_window(2 * p - 2, 2 * p - 1, 8 + kp)
            for kp in range(STEPS):
                if kp == 0:
                    hg_read_q(2 * p, base, first)
                lead(base + 1, kp)
                hg_window(2 * p, 0, kp, A_GEN, {}, first)
            for kp in range(STEPS):
                if kp == 0:
                    read_banks(base + 1, (g_v[:, 0:2, :], g_v[:, 2:4, :]), (0, 1))
                hg_chunks(2 * p, 8 + kp, A_SCORE, A_APPLY)
                lead(base + 2, kp)
                hg_window(2 * p, 0, 8 + kp, A_GEN, {})
            for kp in range(STEPS):
                if kp == 0:
                    hg_read_q(2 * p + 1, base + 2)
                hg_chunks(2 * p, 16 + kp, A_SCORE, A_APPLY)
                hg_chunks(2 * p + 1, kp, B_SCORE, B_APPLY)
                lead(base + 3, kp)
                hg_window(2 * p, 0, 16 + kp, {}, A_NORM)
                hg_window(2 * p + 1, 1, kp, B_GEN, {})

        pair(0, True)
        with dve.Fori(1, PAIRS) as p:
            pair(p, False)

        def out_lead(blk, k, last=False):
            k2 = k + LEAD
            if k2 < BSTEPS:
                w_lo(out_step(blk, k2))
            elif not last:
                w_lo(out_step(blk + 1, k2 - BSTEPS))

        def make_z(blk, nb):
            for b in range(4):
                dve.wait_ge(bank_done[b], blk + (PANELS + 1))
                tt(z[:, b, ds(nb * 512, 512)], main[:, b, :], gate_bc[:, ds(nb * 512, 512)],
                   ALU.mult).then_inc(bank_read[b], 1)
            for b in range(4):
                dve.wait_ge(bank_read[b], blk + (PANELS + 1))
                dve.wait_ge(xre_in[b], blk * 16 + 16)
                zs = z[:, b, ds(nb * 512, 512)]
                stt(out=zs, in0=x_re[:, b, :], scalar=ALPHA, in1=zs, op0=ALU.mult, op1=ALU.add).then_inc(z_made, 1)

        zst = tmp_s[:, 0:96]

        def z_moments(i, half):
            dve.wait_ge(z_made, (half + 1) * 16)
            for j in range(4):
                nc.vector.bn_stats(zst[:, 24 * i + 6 * j:24 * i + 6 * j + 6], z[:, i, j * 512:(j + 1) * 512])
            dve.drain()
            nc.vector.bn_aggr(stats[:, 32 + 2 * i:34 + 2 * i], zst[:, 24 * i:24 * i + 24]).then_inc(zvar_ready, 1)

        def z_finish(i, half):
            dve.wait_ge(zrstd_ready, half * 4 + i + 1)
            ts(z[:, i, :], z[:, i, :], stats[:, 32 + 2 * i:33 + 2 * i], stats[:, 33 + 2 * i:34 + 2 * i],
                        ALU.subtract, ALU.mult)
            dve.drain()
            tt(quarters(z[:, i, :]), quarters(z[:, i, :]), lnw_bc, ALU.mult).then_inc(z_scaled, 1)

        hg_read_g(PANELS - 1, HG_HEADS - 2)
        for k in range(BSTEPS):
            if k % 2:
                hg_chunks(HG_HEADS - 1, 8 + k // 2, B_SCORE, B_APPLY)
            out_lead(0, k)
            if k % 2:
                tail_window(HG_HEADS - 2, HG_HEADS - 1, 8 + k // 2, True)
        dve.wait_ge(gatebc_in, 16)
        make_z(0, 0)
        with dve.Fori(1, 4) as nb:
            for k in range(BSTEPS):
                out_lead(nb, k)
            make_z(nb, nb)
        for k in range(BSTEPS):
            out_lead(4, k)
            if k < 4:
                z_moments(k, 0)
            if k == 4:
                dve.wait_ge(lnwb_in, 32)
            if k in (4, 6, 8, 10):
                z_finish(k // 2 - 2, 0)
        dve.wait_ge(out_stored, 64)
        make_z(4, 0)
        with dve.Fori(1, 3) as nb:
            for k in range(BSTEPS):
                out_lead(nb + 4, k)
            make_z(nb + 4, nb)
        for k in range(BSTEPS):
            out_lead(7, k, True)
        make_z(7, 3)
        for i in range(4):
            z_moments(i, 1)
            z_finish(i, 1)

    @block.gpsimd
    def _(pool):
        tt = nc.gpsimd.tensor_tensor
        nc.gpsimd.memset(smalls[:], 0.0)
        nc.gpsimd.memset(ones[:], 1.0)
        nc.gpsimd.memset(eps_t, EPS)
        pool.drain()
        nc.gpsimd.memset(stats[:, 60:61], 0.0).then_inc(set_up, 1)
        pool.wait_ge(mod_done, 1)
        pool.dma_start(decay_m[:], table_dram[:, P:5 * P]).then_inc(decay_in, 16)
        pool.dma_start(q_decay_m[:], table_dram[:, 5 * P:9 * P]).then_inc(decay_in, 16)
        pool.wait_ge(sums_zero, 2)
        pool.dma_start(gate_sum[0:1, :], b_ada[:, 2 * D:3 * D]).then_inc(gate_bias_in, 16)
        for k in range(NK):
            if k >= 2:
                pool.wait_ge(gate_used, k - 1)
            pool.dma_start(gate_in[k % 2][:], w_ada_k[:, k, 2 * D:3 * D]).then_inc(gate_loaded[k % 2], 16)
        pool.wait_ge(gate_copied, 1)
        pool.dma_start(gate_dram, gate_out[0:1, :]).then_inc(gate_stored, 16)

        def ret_qx(r):
            pool.wait_ge(rope_ready, r + 1)
            if isinstance(r, int):
                pool.wait_ge(decay_in, 32)
            for c in range(8):
                cs = slice(c * P, (c + 1) * P)
                last = tt(r_qx[:, cs], r_q[:, cs], q_decay_m[:, ds(r, 1), :].rearrange("p a n -> p (a n)"), ALU.mult)
            last.then_inc(qx_ready, 1)

        def store(mix, tile, half, o, done):
            pool.wait_ge(mlo_ready, mix + 1)
            hs = slice(half * 512, (half + 1) * 512)
            dst_hi = mix_hi_dram[ds(tile, 1), :, hs].rearrange("a p n -> p (a n)")
            dst_lo = mix_lo_dram[ds(tile, 1), :, hs].rearrange("a p n -> p (a n)")
            pool.dma_start(dst_hi, tmp_hi[:].bitcast(F32)).then_inc(done, 16)
            pool.dma_start(dst_lo, o).then_inc(done, 16)

        def ret_after(r):
            for half in range(2):
                pool.wait_ge(o_copied, ret_chunk(r, 8))
                if half:
                    pool.wait_ge(ssum_done, ret_norm(r, half))
                else:
                    pool.wait_ge(rope_ready, r + 1)
                hs = slice(half * 512, (half + 1) * 512)
                tt(r_t[:, 0:512], r_o[:, 0, hs], r_o[:, 0, hs], ALU.mult)
                tt(r_t[:, 512:T], r_o[:, 1, hs], r_o[:, 1, hs], ALU.mult).then_inc(sq_ready, 1)
            for half in range(2):
                for e in range(2):
                    store(ret_mix(r, half, e), 2 * r + e, half, r_o[:, e, half * 512:(half + 1) * 512], mix_stored)

        ret_qx(0)
        with pool.Fori(1, RET_HEADS) as r:
            ret_after(r - 1)
            ret_qx(r)
        ret_after(RET_HEADS - 1)

        def hg_levels(n, u):
            buf = u % 2
            us = slice(u * 256, (u + 1) * 256)
            pool.wait_ge(lev_exps, n * 4 + (u + 1))
            q, k = g_q[:, us], g_k[:, us]
            for i, m in enumerate(LEVELS):
                lv = lev[:, buf, i, :].rearrange("p (n h m) -> p n h m", h=2, m=m)
                kv = k.rearrange("p (n h m) -> p n h m", h=2, m=m)
                qv = q.rearrange("p (n h m) -> p n h m", h=2, m=m)
                tt(lv[:, :, 0, :], lv[:, :, 0, :], kv[:, :, 0, :], ALU.mult)
                tt(lv[:, :, 1, :], lv[:, :, 1, :], qv[:, :, 1, :], ALU.mult)
            tt(qe[:, buf, :], qe[:, buf, :], q, ALU.mult)
            tt(lev[:, buf, NL, :], lev[:, buf, NL, :], k, ALU.mult).then_inc(lev_ready, 1)

        def hg_squares(n, side, half, free):
            pool.wait_ge(o_copied, hg_chunk(n, 4 * half + 4))
            pool.wait_ge(ssum_done, hg_norm(n, half))
            pool.wait_ge(mix_stored, free)
            hs = slice(half * 512, (half + 1) * 512)
            tt(tmp_s[:], g_o[:, side, hs], g_o[:, side, hs], ALU.mult).then_inc(sq_ready, 1)

        def hg_store(n, side, half, done):
            store(hg_mix(n, half), 8 + n, half, g_o[:, side, half * 512:(half + 1) * 512], done)

        def window(n_a, n_b, w):
            if w + 16 in A_NORM:
                hg_squares(n_a, 0, A_NORM[w + 16], n_a * 64 + 32 * 16)
            for u, at_ in B_GEN.items():
                if at_ == w:
                    hg_levels(n_b, u)

        def tail_window(n_a, n_b, w, tail):
            if w in B_NORM:
                if tail:
                    hg_squares(n_b, 1, B_NORM[w], n_a * 64 + 32 * 16)
                else:
                    hg_squares(n_b, 1, B_NORM[w], (n_a * 64 + 32 * 16) if B_NORM[w] == 0 else (n_b * 64 + 32 * 17))
            if w + 16 in A_MIX and not tail:
                hg_store(n_a, 0, A_MIX[w + 16], mix_stored)
            if w in B_MIX and not tail:
                hg_store(n_b, 1, B_MIX[w], mix_stored)
            for u, at_ in B_GEN.items():
                if at_ == w:
                    hg_levels(n_b, u)

        def pair(p, first):
            if not first:
                for kp in range(STEPS):
                    tail_window(2 * p - 2, 2 * p - 1, 8 + kp, False)
            for u in range(4):
                hg_levels(2 * p, u)
            for kp in range(STEPS):
                window(2 * p, 2 * p + 1, kp)

        pair(0, True)
        with pool.Fori(1, PAIRS) as p:
            pair(p, False)
        for kp in range(STEPS):
            tail_window(HG_HEADS - 2, HG_HEADS - 1, 8 + kp, True)
            if kp == 4:
                pool.wait_ge(scores_done, hg_chunk(HG_HEADS, 0))
                pool.wait_ge(gate_stored, 16)
                pool.dma_start(gate_bc[:], gate_dram.to_broadcast([P, D])).then_inc(gatebc_in, 16)

        def x_pieces(blk, nb, half):
            for b in range(4):
                if not (isinstance(blk, int) and blk == 0):
                    pool.wait_ge(z_made, blk * 4 + (b - 3))
                src = x_t[:, half * 4 + b, ds(nb * 512, 512)]
                pool.dma_start(x_re[:, b, :], src).then_inc(xre_in[b], 16)

        def finish(half):
            for i in range(4):
                pool.wait_ge(z_scaled, half * 4 + i + 1)
                tt(quarters(z[:, i, :]), quarters(z[:, i, :]), lnb_bc, ALU.add).then_inc(z_done, 1)
                pool.wait_ge(z_done, half * 4 + i + 1)
                pool.dma_start(out_t[:, half * 4 + i, :], z[:, i, :]).then_inc(out_stored, 16)

        x_pieces(0, 0, 0)
        with pool.Fori(1, 4) as nb:
            x_pieces(nb, nb, 0)
        pool.wait_ge(bank_done[3], PANELS + 4)
        pool.dma_start(lnw_bc, ln_w.to_broadcast([P, D]).rearrange("p (a n) -> p a n", a=4)).then_inc(lnwb_in, 16)
        pool.dma_start(lnb_bc, ln_b.to_broadcast([P, D]).rearrange("p (a n) -> p a n", a=4)).then_inc(lnwb_in, 16)
        pool.wait_ge(lnwb_in, 32)
        finish(0)
        with pool.Fori(0, 4) as nb:
            x_pieces(nb + 4, nb, 1)
        finish(1)

    ctx.close()


_INS = ['x', 'c', 'positions', 'w_ada', 'b_ada', 'w_in', 'lb_logits', 'hg_norm_w', 'w_out', 'ln_w', 'ln_b']
_OUTS = [((1, T, D), 'float32')]


def kernel(**inputs):
    import numpy as _np
    import concourse.bacc as _bacc
    from concourse import mybir as _mybir
    from concourse.bass_utils import run_bass_kernel_spmd as _run

    nc = _bacc.Bacc("TRN2", target_bir_lowering=False, num_devices=1)
    arrays, args = {}, []
    for name in _INS:
        a = _np.ascontiguousarray(inputs[name])
        arrays[f"in_{name}_dram"] = a
        args.append(nc.dram_tensor(f"in_{name}_dram", a.shape, _mybir.dt.from_np(a.dtype), kind="ExternalInput").ap())
    for i, (shape, dtype) in enumerate(_OUTS):
        args.append(nc.dram_tensor(f"out_{i}_dram", shape, _mybir.dt.from_np(_np.dtype(dtype)), kind="ExternalOutput").ap())
    hymba_layer(nc, *args)
    r = _run(nc, [arrays], core_ids=[0])
    return r.results[0]["out_0_dram"]
```

```python
from contextlib import ExitStack

import numpy as np

import concourse.bass as bass
from concourse import mybir

ACT = mybir.ActivationFunctionType
ALU = mybir.AluOpType
F32 = mybir.dt.float32
F32R = mybir.dt.float32r
U8 = mybir.dt.uint8
I32 = mybir.dt.int32
ds = bass.ds

P = 128
T, D = 1024, 2048
NT, NK = T // P, D // P
RET_HEADS, RET_DV = 4, 256
HG_HEADS = 8
PAIRS = HG_HEADS // 2
EPS = 1e-6
ALPHA = 2.0 ** 0.25
C_RQ, C_RK, C_RV, C_RG, C_HQ, C_HF, C_HI, C_HG = 0, 512, 1024, 2048, 3072, 4096, 5120, 6144
LEVELS = (64, 32, 16, 8, 4, 2, 1)
NL = len(LEVELS)
STEPS = 8
RING = 4
RET_PANELS = 3 * RET_HEADS
PANELS = RET_PANELS + 4 * PAIRS
BSTEPS = 16
XBUFS = 4
LEAD = 3

A_GEN = {0: 2, 1: 3, 2: 9, 3: 11}
B_GEN = {0: 2, 1: 3, 2: 6, 3: 8}
A_SCORE = {7: 0, 8: 1, 9: 2, 10: 3, 12: 4, 13: 5, 14: 6, 15: 7}
B_SCORE = {4: 0, 5: 1, 6: 2, 7: 3, 9: 4, 10: 5, 11: 6, 12: 7}
A_APPLY = {s + 1: c for s, c in A_SCORE.items()}
B_APPLY = {s + 1: c for s, c in B_SCORE.items()}
A_NORM, A_MIX = {17: 0, 18: 1}, {25: 0, 26: 1}
B_NORM, B_MIX = {8: 0, 13: 1}, {11: 0, 14: 1}


def constants():
    i = np.arange(P)
    gamma = 1.0 - 2.0 ** -(5.0 + 7.0 * np.arange(RET_HEADS) / (RET_HEADS - 1))
    scale = float(P) ** -0.5
    diff = (i[None, :] - i[:, None]).astype(np.float64)
    decay = [np.where(diff >= 0, g ** np.maximum(diff, 0), 0.0) * scale for g in gamma]
    q_decay = [np.broadcast_to(g ** (i + 1.0) * scale, (P, P)) for g in gamma]
    k_decay = np.stack([g ** (P - 1.0 - i) for g in gamma], 1)
    chunk_decay = np.broadcast_to(gamma ** float(P), (P, RET_HEADS))
    freq = (10000.0 ** (-np.arange(64) / 64.0))[i % 64][:, None]
    sign = np.where(i < 64, 1.0, -1.0)[:, None]
    table = np.concatenate([np.eye(P), *decay, *q_decay, k_decay, chunk_decay, freq, sign], 1).astype(np.float32)
    s, t = i[:, None], i[None, :]
    masks = [((s // (2 * m) == t // (2 * m)) & (s // m % 2 == 0) & (t // m % 2 == 1)) for m in LEVELS[1:]]
    return np.ascontiguousarray(table), np.ascontiguousarray(np.concatenate(masks, 1).astype(np.uint8))


def hymba_layer(nc, x, c, positions, w_ada, b_ada, w_in, lb_logits, hg_norm_w, w_out, ln_w, ln_b, out):
    table_np, masks_np = constants()
    table_dram = nc.inline_tensor(table_np, "shape_tables").ap()
    masks_dram = nc.inline_tensor(masks_np, "level_masks").ap()
    mix_hi_dram = nc.dram_tensor("mixed_hi", (NK, P, T), F32, kind="Internal").ap()
    mix_lo_dram = nc.dram_tensor("mixed_lo", (NK, P, T), F32, kind="Internal").ap()
    gate_dram = nc.dram_tensor("gate_row", (1, D), F32, kind="Internal").ap()

    start = (nc.sbuf_base + 63) // 64 * 64

    def place(name, at, shape, dt=F32):
        size = (int(np.prod(shape[1:])) * (1 if dt == U8 else 4) + 31) // 32 * 32
        assert start + at + size <= nc.sbuf_usable_end, (name, start + at + size - nc.sbuf_usable_end)
        return nc.alloc_sbuf_tensor_at(name, list(shape), dt, offset=start + at), at + size

    KB = 1024
    h_hi, at = place("h_hi", 0, [P, NK, T], F32R)
    h_lo, at = place("h_lo", at, [P, NK, T], F32R)
    H_LO = 64 * KB
    x_in = [place(f"x_in{i}", i * 8 * KB, [P, D])[0] for i in range(XBUFS)]
    angle = place("angle", 48 * KB, [P, T])[0]
    turns = place("turns", 52 * KB, [P, T])[0]
    pos_i = place("pos_i", 56 * KB, [P, T], I32)[0]
    part_t = place("part_t", 56 * KB, [P, T])[0]
    smalls = place("smalls", 60 * KB, [P, P])[0]
    lnx_t = place("lnx_t", H_LO, [P, NK, T])[0]
    w_raw, _ = place("w_raw", at, [P, RING, 512])
    w_low, at = place("w_low", at, [P, RING, 512], F32R)
    w_high, at = place("w_high", at, [P, RING, 512], F32R)
    ident, at = place("ident", at, [P, P])
    ones, at = place("ones", at, [P, P])
    smalls_t, at = place("smalls_t", at, [P, 40])
    vecs, at = place("vecs", at, [P, 96])
    stats, at = place("stats", at, [P, 64])
    cond = vecs[:, 0:16]
    shift_t, scale1_t = vecs[:, 16:32], vecs[:, 32:48]
    lower, upper = vecs[:, 48:56], vecs[:, 56:64]
    lbtmp = vecs[:, 64:80]
    eps_t = vecs[:, 80:81]
    one_t = ones[:, 0:1]
    half_pi = vecs[:, 81:82]
    freq_t, sign_t = vecs[:, 82:83], vecs[:, 83:84]
    k_decay, chunk_decay = vecs[:, 84:88], vecs[:, 88:92]
    ln_upper = vecs[:, 64:72]
    head_vecs = vecs[:, 92:96]
    at_buf, at = place("at_buf", at, [P, 2, P])
    kt_buf, at = place("kt_buf", at, [P, 2, P])
    state, at = place("state", at, [P, RET_DV])
    tmp_hi, _ = place("tmp_hi", at, [P, 512], F32R)
    TMP0 = at
    tmp_s, at = place("tmp_s", at, [P, 512])
    tmp_e, at = place("tmp_e", at, [P, 512])
    masks, at = place("masks", at, [P, (NL - 1) * P], U8)
    dec_t, at = place("dec_t", at, [P, 2, 2])
    ada_bias = tmp_e[:, 0:32]
    A0 = at
    r_q, at = place("r_q", A0, [P, T])
    r_k, at = place("r_k", at, [P, T])
    r_qx, at = place("r_qx", at, [P, T])
    r_t, at = place("r_t", at, [P, T])
    V0 = at
    r_v, at = place("r_v", at, [P, NT, RET_DV])
    r_g, at = place("r_g", at, [P, 2, T])
    r_o, at = place("r_o", at, [P, 2, T])
    cos_t, at = place("cos_t", at, [P, T])
    sin_t, at = place("sin_t", at, [P, T])
    decay_m, at = place("decay_m", at, [P, RET_HEADS, P])
    q_decay_m, at = place("q_decay_m", at, [P, RET_HEADS, P])
    ada_in = [place(f"ada_in{i}", o, [P, 4, 512])[0] for i, o in enumerate((V0, V0 + 8 * KB, V0 + 16 * KB, A0 + 8 * KB))]
    ada_sum = [[place(f"ada_sum{i}{j}", o, [P, 512])[0] for j, o in enumerate(pair)]
               for i, pair in enumerate(((V0 + 32 * KB, V0 + 34 * KB), (A0 + 52 * KB, TMP0)))]
    h_tmp = place("h_tmp", A0, [P, 2, T])[0]
    gate_in = [place(f"gate_in{i}", V0 + 4 * KB * i, [P, D // 2])[0] for i in range(4)]
    gate_sum = place("gate_sum", V0 + 16 * KB, [P, D])[0]
    gate_out = place("gate_out", V0 + 8 * KB, [P, D])[0]
    g_q, at = place("g_q", A0, [P, T])
    g_k, at = place("g_k", at, [P, T])
    g_b, at = place("g_b", at, [P, T])
    Z0 = at
    g_v, at = place("g_v", at, [P, NT, 256])
    g_g, at = place("g_g", at, [P, 2, T])
    g_o, at = place("g_o", at, [P, 2, T])
    lev, at = place("lev", at, [P, 2, NL + 1, 256])
    qe, at = place("qe", at, [P, 2, 256])
    gate_bc = place("gate_bc", A0, [P, D])[0]
    z, at = place("z", Z0, [P, 4, D])
    x_re, at = place("x_re", at, [P, 4, 512])
    late = place("late", 0, [P, NK, T])[0]
    lnw_bc, lnb_bc = late[:, 0:4, 0:512], late[:, 4:8, 0:512]

    main = nc.alloc_psum_tensor("main", [P, 4, 512], F32)
    sc0 = nc.alloc_psum_tensor("sc0", [P, 512], F32)
    sc1 = nc.alloc_psum_tensor("sc1", [P, 512], F32)
    ops = nc.alloc_psum_tensor("ops", [P, 512], F32)
    aux = nc.alloc_psum_tensor("aux", [P, 512], F32)

    z_banks = ([main[:, b, :] for b in range(4)], [sc0[:], sc1[:], ops[:], aux[:]])

    ctx = ExitStack()

    def sem(name):
        return ctx.enter_context(nc.semaphore(name))

    tables_in, smalls_in, pos_in = sem("tables_in"), sem("smalls_in"), sem("pos_in")
    decay_in, gate_bias_in = sem("decay_in"), sem("gate_bias_in")
    x_loaded = [sem(f"x_loaded{i}") for i in range(XBUFS)]
    ada_loaded = [sem(f"ada_loaded{i}") for i in range(4)]
    gate_loaded = [sem(f"gate_loaded{i}") for i in range(4)]
    set_up = sem("set_up")
    x_stats = sem("x_stats")
    x_normed = sem("x_normed")
    x_turned = sem("x_turned")
    x_placed = sem("x_placed")
    smalls_turned, smalls_placed = sem("smalls_turned"), sem("smalls_placed")
    cond_exp, cond_ready, lb_diff, lb_exp = sem("cond_exp"), sem("cond_ready"), sem("lb_diff"), sem("lb_exp")
    lb_ready, ln_ready = sem("lb_ready"), sem("ln_ready")
    sums_zero = sem("sums_zero")
    ada_used = sem("ada_used")
    mod_done = sem("mod_done")
    mod_ready = sem("mod_ready")
    h_last = sem("h_last")
    angle_ready, trig_ready = sem("angle_ready"), sem("trig_ready")
    h_made = sem("h_made")
    h_ready = sem("h_ready")
    gate_used, gate_turned, gate_copied, gate_stored = (
        sem("gate_used"), sem("gate_turned"), sem("gate_copied"), sem("gate_stored"))
    w_loaded = [sem(f"w_loaded{i}") for i in range(RING)]
    w_hi_ready, w_lo_ready = sem("w_hi_ready"), sem("w_lo_ready")
    w_used = sem("w_used")
    bank_done = [sem(f"bank_done{i}") for i in range(4)]
    bank_read = [sem(f"bank_read{i}") for i in range(4)]
    rope_ready, qx_ready = sem("rope_ready"), sem("qx_ready")
    head_ready = sem("head_ready")
    logf_ready = sem("logf_ready")
    b_ready = sem("b_ready")
    lev_args, lev_exps, lev_ready = sem("lev_args"), sem("lev_exps"), sem("lev_ready")
    scores_done, at_ready, pv_done, o_copied = sem("scores_done"), sem("at_ready"), sem("pv_done"), sem("o_copied")
    kt_done, kt_copied, kv_done, state_ready = sem("kt_done"), sem("kt_copied"), sem("kv_done"), sem("state_ready")
    sq_parts = sem("sq_parts")
    sq_ready, ssum_done, ssum_read, rstd_ready, o_normed = (
        sem("sq_ready"), sem("ssum_done"), sem("ssum_read"), sem("rstd_ready"), sem("o_normed"))
    gate_ready, silu_done, mixed_ready, mhi_ready, mlo_ready = (
        sem("gate_ready"), sem("silu_done"), sem("mixed_ready"), sem("mhi_ready"), sem("mlo_ready"))
    mix_stored = sem("mix_stored")
    mix_in = [sem(f"mix_in{i}") for i in range(NK - 2)]
    mix_late = sem("mix_late")
    gatebc_in, lnwb_in = sem("gatebc_in"), sem("lnwb_in")
    xre_in = [sem(f"xre_in{i}") for i in range(4)]
    z_made = sem("z_made")
    z_scaled, z_normed, z_shifted, out_stored = sem("z_scaled"), sem("z_normed"), sem("z_shifted"), sem("out_stored")
    z_summed = sem("z_summed")
    zvar_ready = sem("zvar_ready")

    block = ctx.enter_context(nc.Block())

    LAST_MIX = 4 * RET_HEADS + 2 * (HG_HEADS - 2)

    def in_step(panel, k):
        return panel * STEPS + (k + 1), k % RING, panel * 2 + (k // RING + 1)

    def out_step(blk, k):
        return blk * BSTEPS + (PANELS * STEPS + k + 1), k % RING, blk * 4 + (PANELS * 2 + k // RING + 1)

    def ret_chunk(r, c):
        return r * 8 + c

    def hg_chunk(n, c):
        return n * 8 + (8 * RET_HEADS + c)

    def ret_upd(r, c):
        return r * 7 + c

    def hg_upd(n, c):
        return n * 7 + (7 * RET_HEADS + c)

    def ret_norm(r, half):
        return r * 2 + half

    def hg_norm(n, half):
        return n * 2 + (2 * RET_HEADS + half)

    def ret_mix(r, half, e):
        return r * 4 + (2 * half + e)

    def hg_mix(n, half):
        return n * 2 + (4 * RET_HEADS + half)

    def quarters(row):
        return row.rearrange("p (a n) -> p a n", a=4)

    def start_leads(j):
        return (0, 1) if j == 0 else (j + 1,)

    w_in_k = w_in[0].rearrange("(k p) n -> p k n", p=P)
    w_out_k = w_out[0].rearrange("(k p) n -> p k n", p=P)
    w_ada_k = w_ada[0].rearrange("(k p) n -> p k n", p=P)
    x_t = x[0].rearrange("(t p) n -> p t n", p=P)
    out_t = out[0].rearrange("(t p) n -> p t n", p=P)

    @block.sync
    def _(sp):
        sp.dma_start(ident[:], table_dram[:, 0:P]).then_inc(tables_in, 16)
        sp.dma_start(vecs[:, 82:84], table_dram[:, 9 * P + 8:9 * P + 10]).then_inc(tables_in, 16)
        sp.dma_start(vecs[:, 84:92], table_dram[:, 9 * P:9 * P + 8]).then_inc(tables_in, 16)
        sp.dma_start(pos_i[:], positions.to_broadcast([P, T])).then_inc(pos_in, 16)
        sp.wait_ge(set_up, 1)
        sp.dma_start(smalls[0:16, :], lb_logits.rearrange("a (h p) -> (a h) p", p=P)).then_inc(smalls_in, 16)
        sp.dma_start(smalls[16:24, :], hg_norm_w.rearrange("a (h p) -> (a h) p", p=P)).then_inc(smalls_in, 16)
        sp.dma_start(smalls[24:40, :], c.rearrange("a (k p) -> (a k) p", p=P)).then_inc(smalls_in, 16)
        sp.dma_start(smalls[40:72, :], b_ada[:, 0:2 * D].rearrange("a (k p) -> (a k) p", p=P)).then_inc(smalls_in, 16)

        def ada(i):
            if i >= 4:
                sp.wait_ge(ada_used, 4 * (i - 3))
            k, j = 4 * (i % 4), i // 4
            cols = w_ada_k[:, k:k + 4, 0:2 * D].rearrange("p k (s n) -> p k s n", s=2)
            for h in range(2):
                sp.dma_start(ada_in[i % 4][:, :, 256 * h:256 * h + 256],
                             cols[:, :, h, 256 * j:256 * j + 256]).then_inc(ada_loaded[i % 4], 16)

        for t in range(NT):
            if t >= XBUFS:
                sp.wait_ge(x_turned, 4 * (t - XBUFS + 1))
            sp.dma_start(x_in[t % XBUFS][:], x_t[:, t, :]).then_inc(x_loaded[t % XBUFS], 16)
            if t >= XBUFS - 1:
                ada(t - XBUFS + 1)
        sp.dma_start(masks[:], masks_dram).then_inc(tables_in, 16)

        def slot_free(panel, k):
            if k >= RING:
                sp.wait_ge(w_used, panel * (STEPS - 1) + (k - RING + 1))
            elif k == RING - 1:
                sp.wait_ge(bank_done[3], panel)
            else:
                sp.wait_ge(w_used, panel * (STEPS - 1) + (k - RING + 2))

        def load_split(col, col2, kp):
            dst = w_raw[:, kp % RING, :].rearrange("p (k n) -> p k n", k=2)
            sp.dma_start(dst[:, :, 0:P], w_in_k[:, 2 * kp:2 * kp + 2, ds(col, P)]).then_inc(w_loaded[kp % RING], 16)
            sp.dma_start(dst[:, :, P:2 * P], w_in_k[:, 2 * kp:2 * kp + 2, ds(col2, P)]).then_inc(w_loaded[kp % RING], 16)

        def load_wide(col, kp):
            dst = w_raw[:, kp % RING, :].rearrange("p (k n) -> p k n", k=2)
            sp.dma_start(dst, w_in_k[:, 2 * kp:2 * kp + 2, ds(col, 2 * P)]).then_inc(w_loaded[kp % RING], 32)

        def panel_loads(panel, first, load):
            for kp in range(first, STEPS):
                slot_free(panel, kp)
                load(kp)

        def qk_load(r, kp):
            load_split(C_RQ + P * r, C_RK + P * r, kp)

        def v_load(r, kp):
            load_wide(C_RV + 256 * r, kp)

        for kp in range(RING):
            qk_load(0, kp)
        for i in range(5, 8):
            ada(i)
        for j in range(2, NK // 2):
            ada(4 * j)
            ada(4 * j + 1)
            if j >= 3:
                sp.wait_ge(w_used, j - 2)
                qk_load(0, j + 1) if j + 1 < STEPS else v_load(0, 0)
            ada(4 * j + 2)
            ada(4 * j + 3)
        panel_loads(1, 1, lambda kp: v_load(0, kp))
        panel_loads(2, 0, lambda kp: load_wide(C_RG, kp))
        with sp.Fori(1, RET_HEADS) as r:
            panel_loads(3 * r, 0, lambda kp: qk_load(r, kp))
            panel_loads(3 * r + 1, 0, lambda kp: v_load(r, kp))
            panel_loads(3 * r + 2, 0, lambda kp: load_wide(C_RG + 256 * r, kp))

        def hg_loads(p, last_behind=None):
            base = 4 * p + RET_PANELS
            panel_loads(base, 0, lambda kp: load_split(C_HQ + 256 * p, C_HF + 256 * p, kp))
            panel_loads(base + 1, 0, lambda kp: load_wide(C_HI + 256 * p, kp))
            panel_loads(base + 2, 0, lambda kp: load_split(256 * p + (C_HQ + P), 256 * p + (C_HF + P), kp))
            panel_loads(base + 3, 0, lambda kp: load_wide(C_HG + 256 * p, kp))

        with sp.Fori(0, PAIRS) as p:
            hg_loads(p)

        def out_slot_free(blk, k):
            if k >= RING:
                sp.wait_ge(w_used, blk * (BSTEPS - 1) + (PANELS * (STEPS - 1) + k - RING + 1))
            elif k == RING - 1:
                sp.wait_ge(bank_done[3], blk + PANELS)
            else:
                sp.wait_ge(w_used, blk * (BSTEPS - 1) + (PANELS * (STEPS - 1) + k - RING + 2))

        def load_out(blk, nb, k):
            sp.dma_start(w_raw[:, k % RING, :], w_out_k[:, k, ds(nb * 512, 512)]).then_inc(w_loaded[k % RING], 32)

        def load_mixed(m, half):
            hs = slice(half * 512, (half + 1) * 512)
            for part, src in ((h_hi, mix_hi_dram), (h_lo, mix_lo_dram)):
                sp.dma_start(part[:, m, hs].bitcast(F32), src[m, :, hs]).then_inc(mix_late if half else mix_in[m], 16)

        def out_loads(blk, nb, behind=None):
            for k in range(BSTEPS):
                out_slot_free(blk, k)
                load_out(blk, nb, k)
                if behind:
                    behind(k)

        def first_half(k):
            for m in (2 * k, 2 * k + 1) if k < RING else (k + RING,):
                if m < NK - 2:
                    sp.wait_ge(w_used, (PANELS - 1) * (STEPS - 1) + m // 2 + 1)
                    load_mixed(m, 0)

        sp.wait_ge(mix_stored, 32 * 28)
        out_loads(0, 0, first_half)
        sp.wait_ge(bank_done[3], PANELS)
        out_loads(1, 1, lambda k: load_mixed(k, 1) if k < NK - 2 else None)
        with sp.Fori(2, 4) as nb:
            out_loads(nb, nb)
        with sp.Fori(0, 4) as nb:
            out_loads(nb + 4, nb)
        sp.wait_ge(out_stored, 16 * NT)
        sp.wait_ge(gate_stored, 16)

    @block.tensor
    def _(pe):
        def mm(*a, **k):
            return nc.tensor.matmul(*a, skip_group_check=True, **k)

        pe.wait_ge(tables_in, 48)
        pe.wait_ge(smalls_in, 64)
        nc.tensor.transpose(sc0[:, 0:P], smalls[:], ident[:]).then_inc(smalls_turned, 1)
        for t in range(NT):
            pe.wait_ge(x_normed, t + 1)
            for b in range(4):
                if t >= 1:
                    pe.wait_ge(x_placed, 4 * (t - 1) + b + 1)
                for j in range(4):
                    k = 4 * b + j
                    last = nc.tensor.transpose(main[:, b, j * P:(j + 1) * P], x_in[t % XBUFS][:, k * P:(k + 1) * P], ident[:])
                last.then_inc(x_turned, 1)

        def mod_sums(j):
            pe.wait_ge(ada_used, 16 * j + 16)
            if j >= 2:
                pe.wait_ge(mod_ready, j - 1)
            elif j == 0:
                pe.wait_ge(smalls_placed, 1)
            for i in range(4):
                for part in range(2):
                    last = mm((sc0, sc1)[j % 2][:, i:i + 1], ada_sum[j % 2][part][:, i * P:(i + 1) * P], ones[:, 0:1],
                              start=(i == 0 and part == 0), stop=(part == 1))
            last.then_inc(mod_done, 1)

        mod_sums(0)
        mod_sums(1)

        parts = ((0, 0), (0, 1), (1, 0))
        w_part, h_part = (w_high, w_low), (h_hi, h_lo)

        def panel(pj, turned, hooks, first=False):
            for kp in range(STEPS):
                count, slot, _ = in_step(pj, kp)
                pe.wait_ge(w_lo_ready, count)
                if first and kp < STEPS - 1:
                    pe.wait_ge(h_ready, 2 * kp + 2)
                elif first:
                    pe.wait_ge(h_last, 2)
                for b in range(4):
                    if kp == 0 and first:
                        if b == 0:
                            pe.wait_ge(x_placed, 4 * NT)
                    elif kp == 0:
                        pe.wait_ge(bank_read[b], pj)
                    for kk in range(2):
                        k = 2 * kp + kk
                        if turned:
                            cc, half = b // 2, b % 2
                            for i, (wp, hp) in enumerate(parts):
                                last = mm(main[:, b, :], w_part[wp][:, slot, kk * 256 + cc * P:kk * 256 + (cc + 1) * P],
                                          h_part[hp][:, k, half * 512:(half + 1) * 512],
                                          start=(k == 0 and i == 0), stop=(k == NK - 1 and i == 2))
                        else:
                            for ti in range(2):
                                t = 2 * b + ti
                                for i, (hp, wp) in enumerate(parts):
                                    last = mm(main[:, b, ti * 256:(ti + 1) * 256], h_part[hp][:, k, t * P:(t + 1) * P],
                                              w_part[wp][:, slot, kk * 256:(kk + 1) * 256],
                                              start=(k == 0 and i == 0 and ti == 0), stop=(k == NK - 1 and i == 2))
                    if kp == STEPS - 1:
                        last.then_inc(bank_done[b], 1)
                    elif b == 3:
                        last.then_inc(w_used, 1)
                    for hook in hooks(kp, b):
                        hook()

        def ret_score(r, c):
            if c == 0:
                pe.wait_ge(rope_ready, r + 1)
                if isinstance(r, int):
                    pe.wait_ge(gate_copied, 1)
            if not (isinstance(r, int) and r == 0 and c == 0):
                pe.wait_ge(at_ready, ret_chunk(r, c))
            cs = slice(c * P, (c + 1) * P)
            mm(sc0[:, 0:P], r_k[:, cs], r_q[:, cs], start=True, stop=True).then_inc(scores_done, 1)

        def ret_kt(r, c):
            cs = slice(c * P, (c + 1) * P)
            if c < 7:
                if not (isinstance(r, int) and r == 0 and c == 0):
                    pe.wait_ge(state_ready, ret_upd(r, c))
                if c == 0 and not isinstance(r, int):
                    pe.wait_ge(ssum_read, ret_norm(r, 0))
                nc.tensor.transpose(aux[:, 0:P], r_k[:, cs], ident[:]).then_inc(kt_done, 1)

        def ret_apply(r, c):
            if c == 0:
                for b in range(4):
                    pe.wait_ge(bank_read[b], 3 * r + 2)
            pe.wait_ge(at_ready, ret_chunk(r, c + 1))
            if not (isinstance(r, int) and r == 0 and c == 0):
                pe.wait_ge(o_copied, ret_chunk(r, c))
            if c:
                pe.wait_ge(state_ready, ret_upd(r, c))
                pe.wait_ge(qx_ready, r + 1)
            for e in range(2):
                es = slice(e * P, (e + 1) * P)
                last = mm(ops[:, es], r_v[:, c, es], at_buf[:, c % 2, :], start=True, stop=(c == 0))
                if c:
                    last = mm(ops[:, es], state[:, es], r_qx[:, c * P:(c + 1) * P], start=False, stop=True)
            last.then_inc(pv_done, 1)
            if c < 7:
                pe.wait_ge(kt_copied, ret_upd(r, c + 1))
                mm(aux[:, P:P + RET_DV], kt_buf[:, c % 2, :], r_v[:, c, :], start=True, stop=True).then_inc(kv_done, 1)

        def ret_ssum(r, half):
            pe.wait_ge(sq_ready, ret_norm(r, half + 1))
            if half == 0:
                pe.wait_ge(state_ready, ret_upd(r, 7))
            else:
                pe.wait_ge(ssum_read, ret_norm(r, half))
            mm(aux[:, :], ones[:], r_t[:, 0:512], start=True, stop=True).then_inc(ssum_done, 1)

        def hg_score(n, side, c):
            u, cc = c // 2, c % 2
            if cc == 0:
                pe.wait_ge(lev_ready, n * 4 + (u + 1))
            pe.wait_ge(at_ready, hg_chunk(n, c))
            for i in range(NL):
                g = lev[:, u % 2, i, cc * P:(cc + 1) * P]
                bank, col = (sc0, i * P) if i < 4 else (sc1, (i - 4) * P)
                if i == 0:
                    mm(sc0[0:64, 64:P], g[:, 0:64], g[:, 64:P], start=True, stop=True)
                else:
                    mm(bank[:, col:col + P], g, g, start=True, stop=True)
            cs = slice(c * P, (c + 1) * P)
            mm(sc1[:, 3 * P:4 * P], g_k[:, cs], g_q[:, cs], start=True, stop=True).then_inc(scores_done, 1)

        def hg_kt(n, side, c):
            u, cc = c // 2, c % 2
            if c < 7:
                pe.wait_ge(state_ready, hg_upd(n, c))
                if c == 0 or (c == 4 and side):
                    pe.wait_ge(ssum_read, hg_norm(n, c // 4))
                nc.tensor.transpose(aux[:, 0:P], lev[:, u % 2, NL, cc * P:(cc + 1) * P], ident[:]).then_inc(kt_done, 1)

        def hg_apply(n, side, c):
            u, cc = c // 2, c % 2
            pe.wait_ge(at_ready, hg_chunk(n, c + 1))
            pe.wait_ge(o_copied, hg_chunk(n, c))
            v = g_v[:, c, side * P:(side + 1) * P]
            last = mm(ops[:, 0:P], v, at_buf[:, c % 2, :], start=True, stop=(c == 0))
            if c:
                pe.wait_ge(state_ready, hg_upd(n, c))
                last = mm(ops[:, 0:P], state[:, 0:P], qe[:, u % 2, cc * P:(cc + 1) * P], start=False, stop=True)
            last.then_inc(pv_done, 1)
            if c < 7:
                pe.wait_ge(kt_copied, hg_upd(n, c + 1))
                mm(aux[:, P:2 * P], kt_buf[:, c % 2, :], v, start=True, stop=True).then_inc(kv_done, 1)

        def hg_ssum(n, half, upd):
            pe.wait_ge(sq_ready, hg_norm(n, half + 1))
            pe.wait_ge(state_ready, upd)
            pe.wait_ge(ssum_read, hg_norm(n, half))
            mm(aux[:, :], ones[:], tmp_s[:], start=True, stop=True).then_inc(ssum_done, 1)

        def hg_hooks(n_a, n_b, w_a, w_b):
            def hooks(kp, b):
                todo = []
                for n, side, w0, score, apply in ((n_a, 0, w_a, A_SCORE, A_APPLY), (n_b, 1, w_b, B_SCORE, B_APPLY)):
                    if w0 is None:
                        continue
                    w = w0 + kp
                    if b == 0 and w in apply:
                        if side == 0 and apply[w] == 0:
                            todo.append(lambda n=n: v_in_place(n))
                        todo.append(lambda n=n, side=side, c=apply[w]: hg_apply(n, side, c))
                    if b == 1 and w in score:
                        todo.append(lambda n=n, side=side, c=score[w]: hg_score(n, side, c))
                    if b == 2 and w in score:
                        todo.append(lambda n=n, side=side, c=score[w]: hg_kt(n, side, c))
                if w_a is not None and b == 3 and w_a + kp in A_NORM:
                    todo.append(lambda half=A_NORM[w_a + kp]: hg_ssum(n_a, half, hg_upd(n_a, 7)))
                if w_b is not None and b == 3 and w_b + kp in B_NORM:
                    half = B_NORM[w_b + kp]
                    todo.append(lambda half=half: hg_ssum(n_b, half, hg_upd(n_b, 4 if half == 0 else 7)))
                return todo
            return hooks

        def v_in_place(n):
            for b in range(4):
                pe.wait_ge(bank_read[b], n * 2 + (RET_PANELS + 2))

        def no_hooks(kp, b):
            return ()

        def ret_hooks_g(r):
            def hooks(kp, b):
                if b == 0 and kp >= 1:
                    return (lambda: ret_apply(r, kp - 1),)
                if b == 1:
                    return (lambda: ret_score(r, kp),)
                if b == 2:
                    return (lambda: ret_kt(r, kp),)
                return ()
            return hooks

        def ret_hooks_after(r):
            def hooks(kp, b):
                if b == 0 and kp == 0:
                    return (lambda: ret_apply(r, 7),)
                if b == 2 and kp in (1, 2):
                    return (lambda: ret_ssum(r, kp - 1),)
                return ()
            return hooks

        def next_mod(kp, b):
            return (lambda: mod_sums(kp + 2),) if b == 3 and kp < STEPS - 2 else ()

        def gate_sums(kp, b):
            if kp == STEPS - 1 and b == 3:
                def work():
                    pe.wait_ge(gate_used, 2 * NK)
                    for j, bank in enumerate((sc0, sc1, ops, aux)):
                        last = mm(bank[:, :], ones[:], gate_sum[:, j * 512:(j + 1) * 512], start=True, stop=True)
                    last.then_inc(gate_turned, 1)
                return (work,)
            return ()

        panel(0, True, next_mod, first=True)
        panel(1, False, gate_sums)
        panel(2, True, ret_hooks_g(0))
        with pe.Fori(1, RET_HEADS) as r:
            panel(3 * r, True, ret_hooks_after(r - 1))
            panel(3 * r + 1, False, no_hooks)
            panel(3 * r + 2, True, ret_hooks_g(r))

        def pair(p, before):
            base = 4 * p + RET_PANELS
            panel(base, True, before)
            panel(base + 1, False, hg_hooks(2 * p, None, 0, None))
            panel(base + 2, True, hg_hooks(2 * p, None, 8, None))
            panel(base + 3, True, hg_hooks(2 * p, 2 * p + 1, 16, 0))

        pair(0, ret_hooks_after(RET_HEADS - 1))
        with pe.Fori(1, PAIRS) as p:
            pair(p, hg_hooks(2 * p - 2, 2 * p - 1, 24, 8))

        def out_block(blk, odd, half, hooks=no_hooks):
            first = isinstance(blk, int)
            for k in range(BSTEPS):
                count, slot, _ = out_step(blk, k)
                pe.wait_ge(w_lo_ready, count)
                if first and blk == 0:
                    if k < NK - 2:
                        pe.wait_ge(mix_in[k], 32)
                    else:
                        pe.wait_ge(mlo_ready, LAST_MIX + (1, 3)[k - NK + 2])
                for b in range(4):
                    if k == 0 and not (first and blk == 1):
                        pe.wait_ge(bank_read[b], blk + PANELS - (0 if first and blk == 0 else 1))
                    elif k == 0 and b == 0:
                        pe.wait_ge(at_ready, hg_chunk(HG_HEADS, 0))
                        pe.wait_ge(o_copied, hg_chunk(HG_HEADS, 0))
                        pe.wait_ge(ssum_read, hg_norm(HG_HEADS, 0))
                    t = half * 4 + b
                    for i, (hp, wp) in enumerate(parts):
                        last = mm(z_banks[odd][b], h_part[hp][:, k, t * P:(t + 1) * P], w_part[wp][:, slot, :],
                                  start=(k == 0 and i == 0), stop=(k == BSTEPS - 1 and i == 2))
                    if k == BSTEPS - 1:
                        last.then_inc(bank_done[b], 1)
                    elif b == 3:
                        last.then_inc(w_used, 1)
                    for hook in hooks(k // 2, 2 * (k % 2) + b // 2) if b % 2 == 1 else ():
                        hook()

        out_block(0, 0, 0, hg_hooks(HG_HEADS - 2, HG_HEADS - 1, 24, 8))
        out_block(1, 1, 0)
        out_block(2, 0, 0)
        out_block(3, 1, 0)
        pe.wait_ge(mlo_ready, LAST_MIX + 4)
        pe.wait_ge(mix_late, 32 * (NK - 2))
        with pe.Fori(2, 4) as j:
            out_block(2 * j, 0, 1)
            out_block(2 * j + 1, 1, 1)

    @block.scalar
    def _(act):
        fn = nc.scalar.activation

        nc.scalar.preload_act_table_set("natural_log_exp_and_others")
        act.wait_ge(smalls_turned, 1)
        fn(smalls_t[:], sc0[:, 0:40], ACT.Copy)
        fn(ada_bias, sc0[:, 40:72], ACT.Copy).then_inc(smalls_placed, 1)
        act.wait_ge(smalls_placed, 1)
        fn(cond, smalls_t[:, 24:40], ACT.Exp, scale=-1.0).then_inc(cond_exp, 1)
        act.wait_ge(lb_diff, 1)
        fn(lbtmp, lbtmp, ACT.Exp).then_inc(lb_exp, 1)
        act.wait_ge(lb_ready, 1)
        fn(ln_upper, ln_upper, ACT.Ln).then_inc(ln_ready, 1)
        def x_norm(t):
            act.wait_ge(x_stats, t + 1)
            m, v = stats[:, 2 * t:2 * t + 1], stats[:, 2 * t + 1:2 * t + 2]
            fn(v, v, ACT.Ln, bias=eps_t)
            act.drain()
            fn(v, v, ACT.Exp, scale=-0.5)
            act.drain()
            fn(m, m, ACT.Copy, scale=v)
            act.drain()
            fn(m, m, ACT.Copy, scale=-1.0)
            act.drain()
            fn(x_in[t % XBUFS][:], x_in[t % XBUFS][:], ACT.Identity, bias=m, scale=v).then_inc(x_normed, 1)

        x_norm(0)
        for t in range(NT):
            if t < NT - 1:
                x_norm(t + 1)
            for b in range(4):
                act.wait_ge(x_turned, 4 * t + b + 1)
                fn(lnx_t[:, 4 * b:4 * b + 4, t * P:(t + 1) * P],
                   main[:, b, :].rearrange("p (k n) -> p k n", k=4), ACT.Copy).then_inc(x_placed, 1)
        act.wait_ge(angle_ready, 1)
        fn(turns[:], angle[:], ACT.Abs)
        act.drain()
        fn(cos_t[:], turns[:], ACT.Sin, bias=half_pi, scale=-1.0)
        fn(sin_t[:], angle[:], ACT.Sin)
        act.drain()
        fn(sin_t[:], sin_t[:], ACT.Copy, scale=sign_t).then_inc(trig_ready, 1)
        nc.scalar.preload_act_table_set("natural_log_exp_and_others")

        def w_hi(step):
            count, slot, use = step
            act.wait_ge(w_loaded[slot], use * 32)
            fn(w_high[:, slot, :], w_raw[:, slot, :], ACT.Copy).then_inc(w_hi_ready, 1)

        def lead(pj, k):
            if k < STEPS - 1:
                w_hi(in_step(pj, k + LEAD) if k + LEAD < STEPS else in_step(pj + 1, k + LEAD - STEPS))

        def last_lead(pj):
            w_hi(in_step(pj + 1, LEAD - 1))

        def start_step(k):
            return in_step(k // STEPS, k % STEPS)

        for j in range(NK // 2):
            for k in start_leads(j):
                w_hi(start_step(k))
            act.wait_ge(mod_ready, j + 1)
            for k in (2 * j, 2 * j + 1):
                if k >= 2:
                    act.wait_ge(h_ready, k - 1)
                fn(h_tmp[:, k % 2, :], lnx_t[:, k, :], ACT.Identity, bias=shift_t[:, k:k + 1],
                   scale=scale1_t[:, k:k + 1])
                act.drain()
                fn(h_hi[:, k, :], h_tmp[:, k % 2, :], ACT.Copy).then_inc(h_made, 1)
        w_hi(start_step(STEPS + 1))
        w_hi(start_step(STEPS + 2))

        def read_banks(pj, dsts, banks):
            for b, dst in zip(banks, dsts):
                act.wait_ge(bank_done[b], pj + 1)
                fn(dst, main[:, b, :], ACT.Copy).then_inc(bank_read[b], 1)

        def ret_read_qk(r, pj):
            if isinstance(r, int):
                act.wait_ge(h_ready, NK - 2)
                act.wait_ge(h_last, 2)
            else:
                act.wait_ge(pv_done, ret_chunk(r, 0))
            read_banks(pj, (r_k[:, 0:512], r_k[:, 512:T]), (2, 3))

        def ret_read_v(r, pj):
            if isinstance(r, int):
                act.wait_ge(gate_used, 2 * NK)
            else:
                act.wait_ge(pv_done, ret_chunk(r, 0))
            read_banks(pj, (r_v[:, 4:6, :], r_v[:, 6:8, :]), (2, 3))

        def ret_read_g(r, pj):
            if not isinstance(r, int):
                act.wait_ge(mixed_ready, ret_mix(r, 0, 0))
            read_banks(pj, (r_g[:, 1, 0:512], r_g[:, 1, 512:T]), (2, 3))

        def copy_kt(update, c, scale):
            act.wait_ge(kt_done, update + 1)
            fn(kt_buf[:, c % 2, :], aux[:, 0:P], ACT.Copy, scale=scale).then_inc(kt_copied, 1)

        def ret_chunk_work(r, c_score, c_apply):
            if c_apply is not None:
                act.wait_ge(pv_done, ret_chunk(r, c_apply + 1))
                if c_apply == 0 and not isinstance(r, int):
                    act.wait_ge(mix_stored, ret_mix(r, 0, 0) * 32)
                fn(r_o[:, :, c_apply * P:(c_apply + 1) * P], ops[:, 0:256].rearrange("p (e n) -> p e n", e=2),
                   ACT.Copy).then_inc(o_copied, 1)
            if c_score is not None and c_score < 7:
                copy_kt(ret_upd(r, c_score), c_score, head_vecs[:, 0:1])

        def hg_chunk_work(n, side, c_score, c_apply, o_free=None):
            if c_apply is not None:
                act.wait_ge(pv_done, hg_chunk(n, c_apply + 1))
                if c_apply == 0:
                    act.wait_ge(mix_stored, o_free)
                fn(g_o[:, side, c_apply * P:(c_apply + 1) * P], ops[:, 0:P], ACT.Copy).then_inc(o_copied, 1)
            if c_score is not None and c_score < 7:
                copy_kt(hg_upd(n, c_score), c_score, 1.0)

        def rstd(norm, width):
            act.wait_ge(ssum_done, norm + 1)
            act.wait_ge(o_normed, norm)
            fn(tmp_e[:], aux[:, :], ACT.Ln, scale=1.0 / width, bias=eps_t).then_inc(ssum_read, 1)
            act.wait_ge(ssum_read, norm + 1)
            fn(tmp_e[:], tmp_e[:], ACT.Exp, scale=-0.5).then_inc(rstd_ready, 1)

        def gate_sigmoid(mix, norm, gates):
            act.wait_ge(o_normed, norm)
            if not (isinstance(mix, int) and mix == 0):
                act.wait_ge(silu_done, mix)
            fn(tmp_e[:], gates, ACT.Exp, scale=-1.0)
            act.drain()
            fn(tmp_e[:], tmp_e[:], ACT.Ln, bias=one_t)
            act.drain()
            fn(tmp_e[:], tmp_e[:], ACT.Exp, scale=-1.0).then_inc(gate_ready, 1)

        def mixed_hi(mix, norm, o):
            act.wait_ge(mixed_ready, mix + 1)
            act.wait_ge(ssum_done, norm)
            if not (isinstance(mix, int) and mix == 0):
                act.wait_ge(mix_stored, mix * 32)
            fn(tmp_hi[:], o, ACT.Copy).then_inc(mhi_ready, 1)

        def ret_after(r, kp):
            if kp in (1, 2):
                ret_rstd(r, kp - 1)
            if kp in (3, 4, 5, 6):
                i = kp - 3
                half, e = i // 2, i % 2
                hs = slice(half * 512, (half + 1) * 512)
                gate_sigmoid(ret_mix(r, half, e), ret_norm(r, 2), r_g[:, e, hs])
                mixed_hi(ret_mix(r, half, e), ret_norm(r, 2), r_o[:, e, hs])

        def ret_rstd(r, half):
            norm = ret_norm(r, half)
            act.wait_ge(ssum_done, norm + 1)
            if not (isinstance(r, int) and r == 0 and half == 0):
                act.wait_ge(o_normed, norm)
            if not (isinstance(r, int) and r == 0) and half == 0:
                act.wait_ge(silu_done, ret_mix(r, 0, 0))
            fn(tmp_e[:], aux[:, :], ACT.Ln, scale=1.0 / RET_DV, bias=eps_t).then_inc(ssum_read, 1)
            act.wait_ge(ssum_read, norm + 1)
            fn(tmp_e[:], tmp_e[:], ACT.Exp, scale=-0.5).then_inc(rstd_ready, 1)

        def ret_head(r, first):
            if not first:
                for kp in range(STEPS):
                    if kp == 0:
                        ret_read_g(r - 1, 3 * r - 1)
                        last_lead(3 * r - 1)
                        ret_chunk_work(r - 1, None, 7)
                    lead(3 * r, kp)
                    ret_after(r - 1, kp)
            for kp in range(STEPS):
                if kp == 0:
                    ret_read_qk(r, 3 * r)
                    if not first:
                        last_lead(3 * r)
                lead(3 * r + 1, kp)
                if first and kp == 7:
                    act.wait_ge(gate_turned, 1)
                    for j, bank in enumerate((sc0, sc1, ops, aux)):
                        last = fn(gate_out[0:1, j * 512:(j + 1) * 512], bank[0:1, :], ACT.Copy)
                    last.then_inc(gate_copied, 1)
            for kp in range(STEPS):
                if kp == 0:
                    ret_read_v(r, 3 * r + 1)
                    last_lead(3 * r + 1)
                ret_chunk_work(r, kp, kp - 1 if kp else None)
                lead(3 * r + 2, kp)

        ret_head(0, True)
        act.wait_ge(gate_stored, 16)
        with act.Fori(1, RET_HEADS) as r:
            nc.scalar.preload_act_table_set("natural_log_exp_and_others")
            ret_head(r, False)

        def hg_read_qf(n, pj, first=False):
            if first:
                act.wait_ge(mix_stored, 32 * 16)
                act.wait_ge(pv_done, 8 * RET_HEADS)
            else:
                act.wait_ge(lev_ready, n * 4)
                act.wait_ge(scores_done, hg_chunk(n, 0))
            for b in (2, 3):
                hs = slice((b - 2) * 512, (b - 1) * 512)
                act.wait_ge(bank_done[b], pj + 1)
                fn(g_b[:, hs], main[:, b, :], ACT.Exp, scale=-1.0)
                fn(g_k[:, hs], main[:, b, :], ACT.Exp).then_inc(bank_read[b], 1)
            act.drain()
            fn(g_b[:], g_b[:], ACT.Ln, bias=one_t)
            fn(g_k[:], g_k[:], ACT.Ln, bias=one_t)

        def hg_log(n):
            act.drain()
            fn(g_b[:], g_b[:], ACT.Exp, scale=-1.0)
            act.wait_ge(head_ready, n + 1)
            fn(g_k[:], g_k[:], ACT.Exp, scale=-1.0, bias=head_vecs[:, 3:4])
            act.drain()
            fn(g_b[:], g_b[:], ACT.Ln, scale=head_vecs[:, 1:2], bias=head_vecs[:, 2:3]).then_inc(logf_ready, 1)

        def hg_exps(n, u):
            buf = u % 2
            us = slice(u * 256, (u + 1) * 256)
            if u == 0:
                act.wait_ge(b_ready, n + 1)
            act.wait_ge(lev_args, n * 4 + (u + 1))
            fn(dec_t[:, buf, :], g_b[:, us].rearrange("p (c n) -> p c n", n=P)[:, :, P - 1], ACT.Exp)
            fn(qe[:, buf, :], g_b[:, us], ACT.Exp)
            fn(lev[:, buf, :, :], lev[:, buf, :, :], ACT.Exp).then_inc(lev_exps, 1)

        def hg_chunks(n, side, w, score, apply, o_free):
            c_s, c_a = score.get(w), apply.get(w)
            if c_s is not None or c_a is not None:
                hg_chunk_work(n, side, c_s, c_a, o_free)

        def hg_window(n, w, gen, norm):
            if w == 1:
                hg_log(n)
            if w in norm:
                rstd_hg(n, norm[w])
            for u, at_ in gen.items():
                if at_ == w:
                    hg_exps(n, u)

        def rstd_hg(n, half):
            rstd(hg_norm(n, half), P)

        def hg_mix_work(n, side, half, norm, tail=False):
            hs = slice(half * 512, (half + 1) * 512)
            mix = hg_mix(n, half)
            gate_sigmoid(mix, norm, g_g[:, side, hs])
            if tail:
                act.wait_ge(mixed_ready, mix + 1)
                act.wait_ge(bank_done[3], PANELS)
                fn(h_hi[:, NK - 2 + side, hs], g_o[:, side, hs], ACT.Copy).then_inc(mhi_ready, 1)
            else:
                mixed_hi(mix, norm, g_o[:, side, hs])

        def tail_window(n_a, n_b, w, tail):
            hg_window(n_b, w, B_GEN, B_NORM)
            if w + 16 in A_MIX:
                hg_mix_work(n_a, 0, A_MIX[w + 16], hg_norm(n_b, 1), tail)
            if w in B_MIX:
                hg_mix_work(n_b, 1, B_MIX[w], hg_norm(n_b, B_NORM_DONE[w]), tail)

        B_NORM_DONE = {11: 1, 14: 2}

        def hg_read_g(pj):
            read_banks(pj, (g_g[:, 1, 0:512], g_g[:, 1, 512:T]), (2, 3))

        def pair(p, first):
            base = 4 * p + RET_PANELS
            for kp in range(STEPS):
                if kp == 0:
                    if first:
                        ret_read_g(RET_HEADS - 1, base - 1)
                    else:
                        hg_read_g(base - 1)
                    last_lead(base - 1)
                if first:
                    if kp == 0:
                        ret_chunk_work(RET_HEADS - 1, None, 7)
                else:
                    hg_chunks(2 * p - 1, 1, 8 + kp, B_SCORE, B_APPLY, 0)
                lead(base, kp)
                if first:
                    ret_after(RET_HEADS - 1, kp)
                else:
                    tail_window(2 * p - 2, 2 * p - 1, 8 + kp, False)
            o_free = p * 128 + 32 * 16
            for kp in range(STEPS):
                if kp == 0:
                    hg_read_qf(2 * p, base, first)
                    last_lead(base)
                hg_chunks(2 * p, 0, kp, A_SCORE, A_APPLY, o_free)
                lead(base + 1, kp)
                hg_window(2 * p, kp, A_GEN, {})
            for kp in range(STEPS):
                if kp == 0:
                    read_banks(base + 1, (g_v[:, 4:6, :], g_v[:, 6:8, :]), (2, 3))
                    last_lead(base + 1)
                hg_chunks(2 * p, 0, 8 + kp, A_SCORE, A_APPLY, o_free)
                lead(base + 2, kp)
                hg_window(2 * p, 8 + kp, A_GEN, {})
            for kp in range(STEPS):
                if kp == 0:
                    hg_read_qf(2 * p + 1, base + 2)
                    last_lead(base + 2)
                hg_chunks(2 * p, 0, 16 + kp, A_SCORE, A_APPLY, o_free)
                hg_chunks(2 * p + 1, 1, kp, B_SCORE, B_APPLY, o_free)
                lead(base + 3, kp)
                hg_window(2 * p + 1, kp, B_GEN, {})
                hg_window(2 * p, 16 + kp, {}, A_NORM)

        pair(0, True)
        with act.Fori(1, PAIRS) as p:
            nc.scalar.preload_act_table_set("natural_log_exp_and_others")
            pair(p, False)

        def out_lead(blk, k, last=False):
            k2 = k + LEAD
            if k2 < BSTEPS:
                w_hi(out_step(blk, k2))
            elif not last:
                w_hi(out_step(blk + 1, k2 - BSTEPS))

        hg_read_g(PANELS - 1)
        last_lead(PANELS - 1)
        for k in range(BSTEPS):
            if k % 2:
                hg_chunks(HG_HEADS - 1, 1, 8 + k // 2, B_SCORE, B_APPLY, 0)
            out_lead(0, k)
            if k % 2:
                tail_window(HG_HEADS - 2, HG_HEADS - 1, 8 + k // 2, True)
        with act.Fori(1, 4) as nb:
            for k in range(BSTEPS):
                out_lead(nb, k)

        def z_norm(i):
            act.wait_ge(zvar_ready, i + 1)
            m, v = stats[:, 32 + 2 * (i % 4):33 + 2 * (i % 4)], stats[:, 33 + 2 * (i % 4):34 + 2 * (i % 4)]
            fn(v, v, ACT.Ln, bias=eps_t)
            act.drain()
            fn(v, v, ACT.Exp, scale=-0.5)
            act.drain()
            fn(m, m, ACT.Copy, scale=v)
            act.drain()
            fn(m, m, ACT.Copy, scale=-1.0)
            act.drain()
            fn(z[:, i % 4, :], z[:, i % 4, :], ACT.Identity, bias=m, scale=v).then_inc(z_normed, 1)

        for k in range(BSTEPS):
            out_lead(4, k)
            if k in (5, 6, 7, 8):
                z_norm(k - 5)
        with act.Fori(5, 7) as blk:
            for k in range(BSTEPS):
                out_lead(blk, k)
        for k in range(BSTEPS):
            out_lead(7, k, True)
        for i in range(4, 8):
            z_norm(i)

    @block.vector
    def _(dve):
        tt, ts, stt = nc.vector.tensor_tensor, nc.vector.tensor_scalar, nc.vector.scalar_tensor_tensor

        dve.wait_ge(smalls_placed, 1)
        l0, l1 = smalls_t[:, 0:8], smalls_t[:, 8:16]
        tt(lower, l0, l1, ALU.max)
        dve.drain()
        tt(lbtmp[:, 0:8], l0, lower, ALU.subtract)
        tt(lbtmp[:, 8:16], l1, lower, ALU.subtract)
        dve.drain()
        nc.vector.memset(half_pi, float(np.pi / 2)).then_inc(lb_diff, 1)
        dve.wait_ge(cond_exp, 1)
        ts(cond, cond, 1.0, None, ALU.add)
        dve.drain()
        nc.vector.reciprocal(cond, cond)
        dve.drain()
        tt(cond, cond, smalls_t[:, 24:40], ALU.mult).then_inc(cond_ready, 1)
        dve.wait_ge(lb_exp, 1)
        tt(lower, lbtmp[:, 0:8], lbtmp[:, 8:16], ALU.add)
        dve.drain()
        nc.vector.reciprocal(upper, lower)
        dve.drain()
        tt(lower, lbtmp[:, 0:8], upper, ALU.mult)
        dve.drain()
        ts(upper, lower, -1.0, 1.0, ALU.mult, ALU.add)
        dve.drain()
        ts(ln_upper, upper, 2.0 ** -60, None, ALU.max)
        ts(lower, lower, 2.0 ** -60, None, ALU.max).then_inc(lb_ready, 1)
        dve.wait_ge(cond_ready, 1)

        def ada_add(i):
            dve.wait_ge(ada_loaded[i % 4], 32 * (i // 4 + 1))
            if i % 4 == 0 and i >= 8:
                dve.wait_ge(mod_done, i // 4 - 1)
            for k in range(4):
                w, c_k = ada_in[i % 4][:, k, :], cond[:, 4 * (i % 4) + k:4 * (i % 4) + k + 1]
                acc = ada_sum[(i // 4) % 2][k % 2][:]
                if i % 4 == 0 and k < 2:
                    ts(acc, w, c_k, None, ALU.mult).then_inc(ada_used, 1)
                else:
                    dve.wait_ge(ada_used, 4 * i + k - 1)
                    stt(out=acc, in0=w, scalar=c_k, in1=acc, op0=ALU.mult, op1=ALU.add).then_inc(ada_used, 1)

        for t in range(NT):
            dve.drain()
            dve.wait_ge(x_loaded[t % XBUFS], 16 * (t // XBUFS + 1))
            for j in range(4):
                nc.vector.bn_stats(stats[:, 32 + 6 * j:38 + 6 * j], x_in[t % XBUFS][:, j * 512:(j + 1) * 512])
            dve.drain()
            nc.vector.bn_aggr(stats[:, 2 * t:2 * t + 2], stats[:, 32:56]).then_inc(x_stats, 1)
            if t >= XBUFS:
                ada_add(t - XBUFS)

        def w_lo(step):
            count, slot, _ = step
            dve.wait_ge(w_hi_ready, count)
            tt(w_low[:, slot, :], w_raw[:, slot, :], w_high[:, slot, :].bitcast(F32), ALU.subtract).then_inc(w_lo_ready, 1)

        def lead(pj, k):
            if k < STEPS - 1:
                w_lo(in_step(pj, k + LEAD) if k + LEAD < STEPS else in_step(pj + 1, k + LEAD - STEPS))

        def last_lead(pj):
            w_lo(in_step(pj + 1, LEAD - 1))

        def start_step(k):
            return in_step(k // STEPS, k % STEPS)

        def mod_columns(j):
            dve.wait_ge(mod_done, j + 1)
            sums = (sc0, sc1)[j % 2]
            js = slice(2 * j, 2 * j + 2)
            tt(shift_t[:, js], sums[:, 0:2], ada_bias[:, js], ALU.add)
            stt(out=scale1_t[:, js], in0=sums[:, 2:4], scalar=1.0, in1=ada_bias[:, 16 + 2 * j:18 + 2 * j],
                op0=ALU.add, op1=ALU.add).then_inc(mod_ready, 1)

        for j in range(1, NK // 2):
            for i in range(4 * j, 4 * j + 4):
                ada_add(i)
                if i == 4 * j + 1:
                    mod_columns(j - 1)
                    for k in start_leads(j - 1):
                        w_lo(start_step(k))
        mod_columns(NK // 2 - 1)
        w_lo(start_step(STEPS))
        nc.vector.memset(gate_sum[:], 0.0)
        nc.vector.memset(dec_t[:], 0.0).then_inc(sums_zero, 1)
        for k in (NK - 2, NK - 1):
            dve.wait_ge(h_made, k + 1)
            tt(h_lo[:, k, :], h_tmp[:, k % 2, :], h_hi[:, k, :].bitcast(F32), ALU.subtract).then_inc(h_last, 1)
        w_lo(start_step(STEPS + 1))
        w_lo(start_step(STEPS + 2))

        def gate_add(i):
            k, hs = i // 2, slice((i % 2) * T, (i % 2 + 1) * T)
            dve.wait_ge(gate_loaded[i % 4], 16 * (i // 4 + 1))
            if i < 2:
                dve.wait_ge(gate_bias_in, 16)
            else:
                dve.wait_ge(gate_used, i - 1)
            stt(out=gate_sum[:, hs], in0=gate_in[i % 4][:], scalar=cond[:, k:k + 1], in1=gate_sum[:, hs],
                op0=ALU.mult, op1=ALU.add).then_inc(gate_used, 1)

        GATE_ADDS = (1, 10, 13, 17, 21, 25, 29, 32, 32)
        for i in range(GATE_ADDS[0]):
            gate_add(i)

        def read_banks(pj, dsts, banks):
            for b, dst in zip(banks, dsts):
                dve.wait_ge(bank_done[b], pj + 1)
                nc.vector.tensor_copy(dst, main[:, b, :]).then_inc(bank_read[b], 1)

        def rope(x_, pj, banks):
            for b in banks:
                dve.wait_ge(bank_read[b], pj + 1)
            tt(r_t[0:64, :], x_[64:P, :], sin_t[64:P, :], ALU.mult)
            tt(r_t[64:P, :], x_[0:64, :], sin_t[0:64, :], ALU.mult)
            dve.drain()
            tt(x_[:], x_[:], cos_t[:], ALU.mult)
            dve.drain()

        def rope_q(r, pj):
            dve.wait_ge(trig_ready, 1)
            ts(head_vecs[:, 0:1], k_decay[:, ds(r, 1)], 1.0, None, ALU.mult)
            if not isinstance(r, int):
                dve.wait_ge(ssum_done, ret_norm(r, 0))
            rope(r_q, pj, (0, 1))
            tt(r_q[:], r_q[:], r_t[:], ALU.add)
            dve.drain()

        def rope_k(r, pj):
            rope(r_k, pj, (2, 3))
            tt(r_k[:], r_k[:], r_t[:], ALU.add).then_inc(rope_ready, 1)

        def ret_select(r, c):
            dve.wait_ge(scores_done, ret_chunk(r, c + 1))
            if not (isinstance(r, int) and r == 0 and c < 2):
                dve.wait_ge(pv_done, ret_chunk(r, c - 1))
            if isinstance(r, int) and c == 0:
                dve.wait_ge(decay_in, 32)
            tt(at_buf[:, c % 2, :], sc0[:, 0:P], decay_m[:, ds(r, 1), :].rearrange("p a n -> p (a n)"),
               ALU.mult).then_inc(at_ready, 1)

        def ret_update(r, c):
            dve.wait_ge(kv_done, ret_upd(r, c + 1))
            if c == 0:
                nc.vector.tensor_copy(state[:], aux[:, P:P + RET_DV]).then_inc(state_ready, 1)
            else:
                dve.wait_ge(state_ready, ret_upd(r, c))
                stt(out=state[:], in0=state[:], scalar=chunk_decay[:, ds(r, 1)], in1=aux[:, P:P + RET_DV],
                    op0=ALU.mult, op1=ALU.add).then_inc(state_ready, 1)

        def silu_mul(mix, gates, o, weight):
            dve.wait_ge(gate_ready, mix + 1)
            tt(gates, gates, tmp_e[:], ALU.mult).then_inc(silu_done, 1)
            dve.wait_ge(silu_done, mix + 1)
            if weight is None:
                tt(o, o, gates, ALU.mult).then_inc(mixed_ready, 1)
            else:
                stt(out=o, in0=o, scalar=weight, in1=gates, op0=ALU.mult, op1=ALU.mult).then_inc(mixed_ready, 1)

        def mixed_lo_in_place(mix, side, hs):
            dve.wait_ge(mhi_ready, mix + 1)
            tt(h_lo[:, NK - 2 + side, hs], g_o[:, side, hs], h_hi[:, NK - 2 + side, hs].bitcast(F32),
               ALU.subtract).then_inc(mlo_ready, 1)

        def mixed_lo(mix, o):
            dve.wait_ge(mhi_ready, mix + 1)
            tt(o, o, tmp_hi[:].bitcast(F32), ALU.subtract).then_inc(mlo_ready, 1)

        def ret_after(r, kp):
            if kp in (1, 2):
                half = kp - 1
                hs = slice(half * 512, (half + 1) * 512)
                dve.wait_ge(rstd_ready, ret_norm(r, half + 1))
                tt(r_o[:, 0, hs], r_o[:, 0, hs], tmp_e[:], ALU.mult)
                tt(r_o[:, 1, hs], r_o[:, 1, hs], tmp_e[:], ALU.mult).then_inc(o_normed, 1)
            if kp in (3, 4, 5, 6):
                half, e = (kp - 3) // 2, (kp - 3) % 2
                hs = slice(half * 512, (half + 1) * 512)
                if kp == 3:
                    dve.drain()
                    dve.wait_ge(o_normed, ret_norm(r, 2))
                mix = ret_mix(r, half, e)
                silu_mul(mix, r_g[:, e, hs], r_o[:, e, hs], None)
                mixed_lo(mix, r_o[:, e, hs])

        def ret_read_g(r, pj):
            if not (isinstance(r, int) and r == 0):
                dve.wait_ge(mixed_ready, ret_mix(r, 0, 0))
            read_banks(pj, (r_g[:, 0, 0:512], r_g[:, 0, 512:T]), (0, 1))

        def ret_head(r, first):
            if not first:
                for kp in range(STEPS):
                    if kp == 0:
                        ret_read_g(r - 1, 3 * r - 1)
                        last_lead(3 * r - 1)
                    lead(3 * r, kp)
                    ret_after(r - 1, kp)
            for kp in range(STEPS):
                if kp == 0:
                    if not first:
                        dve.wait_ge(pv_done, ret_chunk(r, 0))
                    read_banks(3 * r, (r_q[:, 0:512], r_q[:, 512:T]), (0, 1))
                    if not first:
                        last_lead(3 * r)
                lead(3 * r + 1, kp)
                if kp == 1:
                    rope_q(r, 3 * r)
                if kp == 2:
                    rope_k(r, 3 * r)
                if first:
                    for i in range(*GATE_ADDS[kp:kp + 2]):
                        gate_add(i)
            for kp in range(STEPS):
                if kp == 0:
                    if first:
                        dve.wait_ge(gate_used, 2 * NK)
                    else:
                        dve.wait_ge(pv_done, ret_chunk(r, 0))
                    read_banks(3 * r + 1, (r_v[:, 0:2, :], r_v[:, 2:4, :]), (0, 1))
                    last_lead(3 * r + 1)
                if kp:
                    ret_update(r, kp - 1)
                ret_select(r, kp)
                lead(3 * r + 2, kp)

        dve.wait_ge(tables_in, 64)
        ret_head(0, True)
        dve.wait_ge(gate_stored, 16)
        with dve.Fori(1, RET_HEADS) as r:
            ret_head(r, False)

        def hg_read_q(n, pj, first=False):
            if first:
                dve.wait_ge(mix_stored, 32 * 16)
                dve.wait_ge(pv_done, 8 * RET_HEADS)
                dve.wait_ge(ln_ready, 1)
            else:
                dve.wait_ge(lev_ready, n * 4)
                dve.wait_ge(scores_done, hg_chunk(n, 0))
            read_banks(pj, (g_q[:, 0:512], g_q[:, 512:T]), (0, 1))
            hg_head(n)

        def hg_head(n):
            ts(head_vecs[:, 1:2], upper[:, ds(n, 1)], 1.0, None, ALU.mult)
            ts(head_vecs[:, 2:3], lower[:, ds(n, 1)], 1.0, None, ALU.mult)
            ts(head_vecs[:, 3:4], ln_upper[:, ds(n, 1)], 1.0, None, ALU.mult).then_inc(head_ready, 1)

        def hg_cumsum(n):
            dve.wait_ge(logf_ready, n + 1)
            for c in range(8):
                cs = slice(c * P, (c + 1) * P)
                last = nc.vector.tensor_tensor_scan(g_b[:, cs], ones[:], g_b[:, cs], 0.0, ALU.mult, ALU.add)
            last.then_inc(b_ready, 1)

        def hg_args(n, u, first=False):
            buf = u % 2
            b = g_b[:, u * 256:(u + 1) * 256]
            if u == 0:
                dve.wait_ge(b_ready, n + 1)
            if not (first and u < 2):
                dve.wait_ge(pv_done, hg_chunk(n, 2 * (u - 1)))
            for i, m in enumerate(LEVELS):
                bv = b.rearrange("p (n h m) -> p n h m", h=2, m=m)
                lv = lev[:, buf, i, :].rearrange("p (n h m) -> p n h m", h=2, m=m)
                mid = bv[:, :, 0, m - 1:m].to_broadcast([P, P // m, m])
                tt(lv[:, :, 0, :], mid, bv[:, :, 0, :], ALU.subtract)
                tt(lv[:, :, 1, :], bv[:, :, 1, :], mid, ALU.subtract)
            bv = b.rearrange("p (c m) -> p c m", m=P)
            tt(lev[:, buf, NL, :].rearrange("p (c m) -> p c m", m=P), bv[:, :, P - 1:P].to_broadcast([P, 2, P]), bv,
               ALU.subtract).then_inc(lev_args, 1)

        def hg_select(n, c):
            dve.wait_ge(scores_done, hg_chunk(n, c + 1))
            dve.wait_ge(pv_done, hg_chunk(n, c - 1))
            a = at_buf[:, c % 2, :]
            tt(a, sc1[:, 3 * P:4 * P], ident[:], ALU.mult)
            dve.drain()
            nc.vector.tensor_copy(a[0:64, 64:P], sc0[0:64, 64:P])
            for i in range(1, NL):
                dve.drain()
                bank, col = (sc0, i * P) if i < 4 else (sc1, (i - 4) * P)
                last = nc.vector.copy_predicated(a, masks[:, (i - 1) * P:i * P], bank[:, col:col + P])
            last.then_inc(at_ready, 1)

        def hg_update(n, c):
            dve.wait_ge(kv_done, hg_upd(n, c + 1))
            if c == 0:
                nc.vector.tensor_copy(state[:, 0:P], aux[:, P:2 * P]).then_inc(state_ready, 1)
            else:
                dve.wait_ge(state_ready, hg_upd(n, c))
                stt(out=state[:, 0:P], in0=state[:, 0:P], scalar=dec_t[:, (c // 2) % 2, c % 2:c % 2 + 1],
                    in1=aux[:, P:2 * P], op0=ALU.mult, op1=ALU.add).then_inc(state_ready, 1)

        def hg_scale_o(n, side, half):
            hs = slice(half * 512, (half + 1) * 512)
            dve.wait_ge(rstd_ready, hg_norm(n, half + 1))
            tt(g_o[:, side, hs], g_o[:, side, hs], tmp_e[:], ALU.mult).then_inc(o_normed, 1)

        def hg_chunks(n, w, score, apply):
            if w in apply and apply[w] < 7:
                hg_update(n, apply[w])
            if w in score:
                hg_select(n, score[w])

        def hg_window(n, side, w, gen, norm, first=False):
            if w == 1:
                hg_cumsum(n)
            if w in norm:
                hg_scale_o(n, side, norm[w])
            for u, at_ in gen.items():
                if at_ == w:
                    hg_args(n, u, first)

        def hg_mix_work(n, side, half, tail):
            hs = slice(half * 512, (half + 1) * 512)
            mix = hg_mix(n, half)
            dve.wait_ge(o_normed, hg_norm(n, half + 1))
            silu_mul(mix, g_g[:, side, hs], g_o[:, side, hs], smalls_t[:, ds(16 + n, 1)])
            if tail:
                mixed_lo_in_place(mix, side, hs)
            else:
                mixed_lo(mix, g_o[:, side, hs])

        def tail_window(n_a, n_b, w, tail=False):
            hg_window(n_b, 1, w, B_GEN, B_NORM)
            if w + 16 in A_MIX:
                hg_mix_work(n_a, 0, A_MIX[w + 16], tail)
            if w in B_MIX:
                hg_mix_work(n_b, 1, B_MIX[w], tail)

        def hg_read_g(pj, n):
            if not isinstance(n, int) or n:
                dve.wait_ge(mixed_ready, hg_mix(n, 0))
            read_banks(pj, (g_g[:, 0, 0:512], g_g[:, 0, 512:T]), (0, 1))

        def pair(p, first):
            base = 4 * p + RET_PANELS
            for kp in range(STEPS):
                if kp == 0:
                    if first:
                        ret_read_g(RET_HEADS - 1, base - 1)
                    else:
                        hg_read_g(base - 1, 2 * p - 2)
                    last_lead(base - 1)
                if not first:
                    hg_chunks(2 * p - 1, 8 + kp, B_SCORE, B_APPLY)
                lead(base, kp)
                if first:
                    ret_after(RET_HEADS - 1, kp)
                else:
                    tail_window(2 * p - 2, 2 * p - 1, 8 + kp)
            for kp in range(STEPS):
                if kp == 0:
                    hg_read_q(2 * p, base, first)
                    last_lead(base)
                hg_chunks(2 * p, kp, A_SCORE, A_APPLY)
                lead(base + 1, kp)
                hg_window(2 * p, 0, kp, A_GEN, {}, first)
            for kp in range(STEPS):
                if kp == 0:
                    read_banks(base + 1, (g_v[:, 0:2, :], g_v[:, 2:4, :]), (0, 1))
                    last_lead(base + 1)
                hg_chunks(2 * p, 8 + kp, A_SCORE, A_APPLY)
                lead(base + 2, kp)
                hg_window(2 * p, 0, 8 + kp, A_GEN, {})
            for kp in range(STEPS):
                if kp == 0:
                    hg_read_q(2 * p + 1, base + 2)
                    last_lead(base + 2)
                hg_chunks(2 * p, 16 + kp, A_SCORE, A_APPLY)
                hg_chunks(2 * p + 1, kp, B_SCORE, B_APPLY)
                lead(base + 3, kp)
                hg_window(2 * p + 1, 1, kp, B_GEN, {})
                hg_window(2 * p, 0, 16 + kp, {}, A_NORM)

        pair(0, True)
        with dve.Fori(1, PAIRS) as p:
            pair(p, False)

        def out_lead(blk, k, last=False):
            k2 = k + LEAD
            if k2 < BSTEPS:
                w_lo(out_step(blk, k2))
            elif not last:
                w_lo(out_step(blk + 1, k2 - BSTEPS))

        zst = tmp_s[:, 0:96]

        def z_piece(blk, odd, nb, b):
            zs = z[:, b, ds(nb * 512, 512)]
            dve.wait_ge(bank_done[b], blk + (PANELS + 1))
            tt(zs, z_banks[odd][b], gate_bc[:, ds(nb * 512, 512)], ALU.mult).then_inc(bank_read[b], 1)
            dve.wait_ge(xre_in[b], blk * 16 + 16)
            dve.wait_ge(bank_read[b], blk + (PANELS + 1))
            stt(out=zs, in0=x_re[:, b, :], scalar=ALPHA, in1=zs, op0=ALU.mult, op1=ALU.add).then_inc(z_made, 1)
            dve.wait_ge(z_made, blk * 4 + (b + 1))
            nc.vector.bn_stats(zst[:, ds(nb * 6 + 24 * b, 6)], zs)

        def z_moments(i, half):
            nc.vector.bn_aggr(stats[:, 32 + 2 * i:34 + 2 * i], zst[:, 24 * i:24 * i + 24]).then_inc(zvar_ready, 1)

        def z_finish(i, half):
            dve.wait_ge(z_normed, half * 4 + i + 1)
            tt(quarters(z[:, i, :]), quarters(z[:, i, :]), lnw_bc, ALU.mult).then_inc(z_scaled, 1)
            if i % 2:
                dve.wait_ge(z_scaled, half * 4 + i + 1)
                tt(quarters(z[:, i, :]), quarters(z[:, i, :]), lnb_bc, ALU.add).then_inc(z_shifted, 1)

        hg_read_g(PANELS - 1, HG_HEADS - 2)
        last_lead(PANELS - 1)
        for k in range(BSTEPS):
            if k % 2:
                hg_chunks(HG_HEADS - 1, 8 + k // 2, B_SCORE, B_APPLY)
            out_lead(0, k)
            if k % 2:
                tail_window(HG_HEADS - 2, HG_HEADS - 1, 8 + k // 2, True)
        dve.wait_ge(gatebc_in, 16)

        def out_leads(blk, odd, nb, last=False):
            for k in range(BSTEPS):
                out_lead(blk, k, last)
                if k < 4:
                    z_piece(blk - 1, 1 - odd, nb, k)

        out_leads(1, 1, 0)
        out_leads(2, 0, 1)
        out_leads(3, 1, 2)
        for k in range(BSTEPS):
            out_lead(4, k)
            if k < 4:
                z_piece(3, 1, 3, k)
            if k == 4:
                dve.drain()
                for i in range(4):
                    z_moments(i, 0)
                dve.wait_ge(lnwb_in, 32)
            if k in (6, 8, 10, 12):
                z_finish(k // 2 - 3, 0)
        dve.wait_ge(out_stored, 64)
        out_leads(5, 1, 0)
        out_leads(6, 0, 1)
        out_leads(7, 1, 2, True)
        for b in range(4):
            z_piece(7, 1, 3, b)
        dve.drain()
        for i in range(4):
            z_moments(i, 1)
        for i in range(4):
            z_finish(i, 1)

    @block.gpsimd
    def _(pool):
        tt = nc.gpsimd.tensor_tensor
        nc.gpsimd.memset(smalls[:], 0.0)
        nc.gpsimd.memset(ones[:], 1.0)
        nc.gpsimd.memset(eps_t, EPS)
        pool.drain()
        nc.gpsimd.memset(stats[:, 60:61], 0.0).then_inc(set_up, 1)
        gts = nc.gpsimd.tensor_scalar
        pool.wait_ge(pos_in, 16)
        pool.wait_ge(tables_in, 48)
        nc.gpsimd.tensor_copy(turns[:], pos_i[:])
        pool.drain()
        gts(angle[:], turns[:], freq_t, None, ALU.mult)
        pool.drain()
        big = 12582912.0
        gts(turns[:], angle[:], float(1.0 / (2.0 * np.pi)), big, ALU.mult, ALU.add)
        pool.drain()
        gts(turns[:], turns[:], big, None, ALU.subtract)
        rest = 2.0 * np.pi
        for unit in (2.0 ** -5, 2.0 ** -13, 2.0 ** -21, None):
            part = float(np.floor(rest / unit) * unit) if unit else float(np.float32(rest))
            rest -= part
            pool.drain()
            gts(part_t[:], turns[:], part, None, ALU.mult)
            pool.drain()
            tt(angle[:], angle[:], part_t[:], ALU.subtract)
        pool.drain()
        gts(angle[:], angle[:], 3.1415925, -3.1415925, ALU.min, ALU.max).then_inc(angle_ready, 1)
        for k in range(NK - 2):
            pool.wait_ge(h_made, k + 1)
            tt(h_lo[:, k, :], h_tmp[:, k % 2, :], h_hi[:, k, :].bitcast(F32), ALU.subtract).then_inc(h_ready, 1)
        pool.wait_ge(mod_done, NK // 2)
        pool.dma_start(decay_m[:], table_dram[:, P:5 * P]).then_inc(decay_in, 16)
        pool.dma_start(q_decay_m[:], table_dram[:, 5 * P:9 * P]).then_inc(decay_in, 16)
        pool.wait_ge(sums_zero, 1)
        pool.dma_start(gate_sum[0:1, :], b_ada[:, 2 * D:3 * D]).then_inc(gate_bias_in, 16)
        for i in range(2 * NK):
            if i >= 4:
                pool.wait_ge(gate_used, i - 3)
            cols = slice(2 * D + (i % 2) * T, 2 * D + (i % 2 + 1) * T)
            pool.dma_start(gate_in[i % 4][:], w_ada_k[:, i // 2, cols]).then_inc(gate_loaded[i % 4], 16)
        pool.wait_ge(gate_copied, 1)
        pool.dma_start(gate_dram, gate_out[0:1, :]).then_inc(gate_stored, 16)

        def ret_qx(r):
            pool.wait_ge(rope_ready, r + 1)
            if isinstance(r, int):
                pool.wait_ge(decay_in, 32)
            for c in range(8):
                cs = slice(c * P, (c + 1) * P)
                last = tt(r_qx[:, cs], r_q[:, cs], q_decay_m[:, ds(r, 1), :].rearrange("p a n -> p (a n)"), ALU.mult)
            last.then_inc(qx_ready, 1)

        def store(mix, tile, half, o, done):
            pool.wait_ge(mlo_ready, mix + 1)
            hs = slice(half * 512, (half + 1) * 512)
            dst_hi = mix_hi_dram[ds(tile, 1), :, hs].rearrange("a p n -> p (a n)")
            dst_lo = mix_lo_dram[ds(tile, 1), :, hs].rearrange("a p n -> p (a n)")
            pool.dma_start(dst_hi, tmp_hi[:].bitcast(F32)).then_inc(done, 16)
            pool.dma_start(dst_lo, o).then_inc(done, 16)

        def ret_after(r):
            for half in range(2):
                pool.wait_ge(o_copied, ret_chunk(r, 8))
                if half:
                    pool.wait_ge(ssum_done, ret_norm(r, half))
                else:
                    pool.wait_ge(rope_ready, r + 1)
                hs = slice(half * 512, (half + 1) * 512)
                tt(r_t[:, 0:512], r_o[:, 0, hs], r_o[:, 0, hs], ALU.mult)
                tt(r_t[:, 512:T], r_o[:, 1, hs], r_o[:, 1, hs], ALU.mult).then_inc(sq_parts, 1)
                pool.wait_ge(sq_parts, ret_norm(r, half + 1))
                tt(r_t[:, 0:512], r_t[:, 0:512], r_t[:, 512:T], ALU.add).then_inc(sq_ready, 1)
            for half in range(2):
                for e in range(2):
                    store(ret_mix(r, half, e), 2 * r + e, half, r_o[:, e, half * 512:(half + 1) * 512], mix_stored)

        ret_qx(0)
        with pool.Fori(1, RET_HEADS) as r:
            ret_after(r - 1)
            ret_qx(r)
        ret_after(RET_HEADS - 1)

        def hg_levels(n, u):
            buf = u % 2
            us = slice(u * 256, (u + 1) * 256)
            pool.wait_ge(lev_exps, n * 4 + (u + 1))
            q, k = g_q[:, us], g_k[:, us]
            for i, m in enumerate(LEVELS):
                lv = lev[:, buf, i, :].rearrange("p (n h m) -> p n h m", h=2, m=m)
                kv = k.rearrange("p (n h m) -> p n h m", h=2, m=m)
                qv = q.rearrange("p (n h m) -> p n h m", h=2, m=m)
                tt(lv[:, :, 0, :], lv[:, :, 0, :], kv[:, :, 0, :], ALU.mult)
                tt(lv[:, :, 1, :], lv[:, :, 1, :], qv[:, :, 1, :], ALU.mult)
            tt(qe[:, buf, :], qe[:, buf, :], q, ALU.mult)
            tt(lev[:, buf, NL, :], lev[:, buf, NL, :], k, ALU.mult).then_inc(lev_ready, 1)

        def hg_squares(n, side, half, free):
            pool.wait_ge(o_copied, hg_chunk(n, 4 * half + 4))
            pool.wait_ge(ssum_done, hg_norm(n, half))
            pool.wait_ge(mix_stored, free)
            hs = slice(half * 512, (half + 1) * 512)
            tt(tmp_s[:], g_o[:, side, hs], g_o[:, side, hs], ALU.mult).then_inc(sq_ready, 1)

        def hg_store(n, side, half, done):
            store(hg_mix(n, half), 8 + n, half, g_o[:, side, half * 512:(half + 1) * 512], done)

        def window(n_a, n_b, w):
            if w + 16 in A_NORM:
                hg_squares(n_a, 0, A_NORM[w + 16], n_a * 64 + 32 * 16)
            for u, at_ in B_GEN.items():
                if at_ == w:
                    hg_levels(n_b, u)

        def tail_window(n_a, n_b, w, tail):
            if w in B_NORM:
                if tail:
                    hg_squares(n_b, 1, B_NORM[w], n_a * 64 + 32 * 16)
                else:
                    hg_squares(n_b, 1, B_NORM[w], (n_a * 64 + 32 * 16) if B_NORM[w] == 0 else (n_b * 64 + 32 * 17))
            if w + 16 in A_MIX and not tail:
                hg_store(n_a, 0, A_MIX[w + 16], mix_stored)
            if w in B_MIX and not tail:
                hg_store(n_b, 1, B_MIX[w], mix_stored)
            for u, at_ in B_GEN.items():
                if at_ == w:
                    hg_levels(n_b, u)

        def pair(p, first):
            if not first:
                for kp in range(STEPS):
                    tail_window(2 * p - 2, 2 * p - 1, 8 + kp, False)
            for u in range(4):
                hg_levels(2 * p, u)
            for kp in range(STEPS):
                window(2 * p, 2 * p + 1, kp)

        pair(0, True)
        with pool.Fori(1, PAIRS) as p:
            pair(p, False)
        for kp in range(STEPS):
            tail_window(HG_HEADS - 2, HG_HEADS - 1, 8 + kp, True)
            if kp == 4:
                pool.wait_ge(scores_done, hg_chunk(HG_HEADS, 0))
                pool.wait_ge(gate_stored, 16)
                pool.dma_start(gate_bc[:], gate_dram.to_broadcast([P, D])).then_inc(gatebc_in, 16)

        def x_pieces(blk, nb, half):
            for b in range(4):
                if not (isinstance(blk, int) and blk == 0):
                    pool.wait_ge(z_made, blk * 4 + (b - 3))
                src = x_t[:, half * 4 + b, ds(nb * 512, 512)]
                pool.dma_start(x_re[:, b, :], src).then_inc(xre_in[b], 16)

        def finish(half):
            for i in range(4):
                if i % 2:
                    pool.wait_ge(z_shifted, half * 2 + (i // 2 + 1))
                else:
                    pool.wait_ge(z_scaled, half * 4 + i + 1)
                    tt(quarters(z[:, i, :]), quarters(z[:, i, :]), lnb_bc, ALU.add).then_inc(z_summed, 1)
                    pool.wait_ge(z_summed, half * 2 + (i // 2 + 1))
                pool.dma_start(out_t[:, half * 4 + i, :], z[:, i, :]).then_inc(out_stored, 16)

        x_pieces(0, 0, 0)
        with pool.Fori(1, 4) as nb:
            x_pieces(nb, nb, 0)
        pool.wait_ge(bank_done[3], PANELS + 4)
        pool.dma_start(lnw_bc, ln_w.to_broadcast([P, D]).rearrange("p (a n) -> p a n", a=4)).then_inc(lnwb_in, 16)
        pool.dma_start(lnb_bc, ln_b.to_broadcast([P, D]).rearrange("p (a n) -> p a n", a=4)).then_inc(lnwb_in, 16)
        pool.wait_ge(lnwb_in, 32)
        finish(0)
        with pool.Fori(0, 4) as nb:
            x_pieces(nb + 4, nb, 1)
        finish(1)

    ctx.close()


_INS = ['x', 'c', 'positions', 'w_ada', 'b_ada', 'w_in', 'lb_logits', 'hg_norm_w', 'w_out', 'ln_w', 'ln_b']
_OUTS = [((1, T, D), 'float32')]


def kernel(**inputs):
    import numpy as _np
    import concourse.bacc as _bacc
    from concourse import mybir as _mybir
    from concourse.bass_utils import run_bass_kernel_spmd as _run

    nc = _bacc.Bacc("TRN2", target_bir_lowering=False, num_devices=1)
    arrays, args = {}, []
    for name in _INS:
        a = _np.ascontiguousarray(inputs[name])
        arrays[f"in_{name}_dram"] = a
        args.append(nc.dram_tensor(f"in_{name}_dram", a.shape, _mybir.dt.from_np(a.dtype), kind="ExternalInput").ap())
    for i, (shape, dtype) in enumerate(_OUTS):
        args.append(nc.dram_tensor(f"out_{i}_dram", shape, _mybir.dt.from_np(_np.dtype(dtype)), kind="ExternalOutput").ap())
    hymba_layer(nc, *args)
    r = _run(nc, [arrays], core_ids=[0])
    return r.results[0]["out_0_dram"]
```
